# Optimizing a Trainium2 kernel written in Bass

```python
import jax, jax.numpy as jnp
from jax import lax
import numpy as np

D_MODEL = 1024
BATCH = 1
SEQ = 1024
DEPTH = 1
DEC_BATCH = 1
DEC_SEQ = 512
PAST_LEN = 128

D_MIX = D_MODEL
D_RWKV = D_MIX // 2
RWKV_HEAD = 64
RWKV_HEADS = D_RWKV // RWKV_HEAD
D_HGRN = D_MIX - D_RWKV
HGRN_HEAD = 128
HGRN_HEADS = D_HGRN // HGRN_HEAD
DECAY_LORA = 64
AAA_LORA = 64
GATE_LORA = 128
HGRN_CHUNK = 32
N_GROUPS = 4
EXPERTS_PER_GROUP = 8
N_EXPERTS = N_GROUPS * EXPERTS_PER_GROUP
TOP_K_IN_GROUP = 2
D_EXPERT = 512
MOE_BLOCK = 128
NORM_EPS = 1e-6
HGRN_NORM_EPS = 1e-5
LNX_EPS = RWKV_HEAD * 1e-5

C_R = 0
C_K = C_R + D_RWKV
C_V = C_K + D_RWKV
C_WD = C_V + D_RWKV
C_AD = C_WD + 2 * DECAY_LORA
C_GD = C_AD + 2 * AAA_LORA
C_RWKV_END = C_GD + GATE_LORA
C_Q = C_RWKV_END
C_F = C_Q + D_HGRN
C_I = C_F + 2 * D_HGRN
C_G = C_I + D_HGRN
D_IN = C_G + D_HGRN

kernel_name = "hymba_rwkv7_hgrn2_hmoe_encoder"

def _rms_norm(x, w, eps=NORM_EPS):
    xf = x.astype(jnp.float32)
    y = xf * lax.rsqrt(jnp.mean(xf * xf, axis=-1, keepdims=True) + eps)
    return (y * w.astype(jnp.float32)).astype(x.dtype)

def _centred_shift(u):
    prev = jnp.pad(u[:, :-1], ((0, 0), (1, 0), (0, 0)))
    nxt = jnp.pad(u[:, 1:], ((0, 0), (0, 1), (0, 0)))
    return 0.5 * (prev + nxt)

def _rwkv7_mixer(u, w0, w2, a0, a2, g2, k_k, k_a, r_k, lnx_w, lnx_b):
    B, T, _ = u.shape
    H, K = RWKV_HEADS, RWKV_HEAD
    f32 = jnp.float32
    r = u[..., C_R:C_K]
    k = u[..., C_K:C_V]
    v = u[..., C_V:C_WD]
    wd = u[..., C_WD:C_AD].reshape(B, T, 2, DECAY_LORA)
    ad = u[..., C_AD:C_GD].reshape(B, T, 2, AAA_LORA)
    gd = u[..., C_GD:C_RWKV_END]
    w_log = -jax.nn.softplus(-(w0[:, None, None, :] + jnp.einsum('btdr,drc->dbtc', jnp.tanh(wd), w2))) - 0.5
    decay = jnp.exp(-jnp.exp(w_log.astype(f32)))
    a = jax.nn.sigmoid(a0[:, None, None, :] + jnp.einsum('btdr,drc->dbtc', ad, a2))
    g = jnp.einsum('btr,rc->btc', jax.nn.sigmoid(gd), g2)
    kk = (k * k_k).reshape(B, T, H, K).astype(f32)
    kk = kk / jnp.maximum(jnp.linalg.norm(kk, axis=-1, keepdims=True), 1e-12)
    kk = kk.reshape(B, T, D_RWKV)
    k_dir = k[None] * (1 + (a - 1) * k_a)
    b_dir = kk[None] * a

    def to_scan(z):
        z = jnp.stack([z[0], jnp.flip(z[1], axis=1)]).astype(f32)
        return jnp.moveaxis(z.reshape(2, B, T, H, K), 2, 0)

    def both(z):
        return to_scan(jnp.broadcast_to(z, (2,) + z.shape))

    xs = (both(r), to_scan(decay), to_scan(k_dir), both(v), both(kk), to_scan(b_dir))

    def step(S, inp):
        r_t, w_t, k_t, v_t, kk_t, b_t = inp
        sa = jnp.einsum('dbhvk,dbhk->dbhv', S, -kk_t)
        S = S * w_t[..., None, :] + sa[..., None] * b_t[..., None, :] + v_t[..., None] * k_t[..., None, :]
        y_t = jnp.einsum('dbhvk,dbhk->dbhv', S, r_t)
        return S, y_t

    S0 = jnp.zeros((2, B, H, K, K), f32)
    _, y = lax.scan(step, S0, xs)
    y = jnp.moveaxis(y, 0, 2)
    y = y[0] + jnp.flip(y[1], axis=1)
    mean = jnp.mean(y, axis=-1, keepdims=True)
    var = jnp.mean(jnp.square(y - mean), axis=-1, keepdims=True)
    y = ((y - mean) * lax.rsqrt(var + LNX_EPS)).reshape(B, T, D_RWKV)
    y = y * lnx_w.astype(f32) + lnx_b.astype(f32)
    bonus = jnp.einsum('bthk,dbthk,hk->bth', r.reshape(B, T, H, K).astype(f32),
                       k_dir.reshape(2, B, T, H, K).astype(f32), r_k.astype(f32))
    y = y + (bonus[..., None] * v.reshape(B, T, H, K).astype(f32)).reshape(B, T, D_RWKV)
    return (y * g.astype(f32)).astype(u.dtype)

def _hgrn2_mixer(u, lb, gnorm_w):
    B, T, _ = u.shape
    H, K, C = HGRN_HEADS, HGRN_HEAD, HGRN_CHUNK
    NC = T // C
    f32 = jnp.float32
    q = jax.nn.silu(u[..., C_Q:C_F].astype(f32))
    f_raw = jnp.moveaxis(u[..., C_F:C_I].reshape(B, T, 2, D_HGRN).astype(f32), 2, 0)
    i_in = u[..., C_I:C_G].astype(f32)
    gate = u[..., C_G:D_IN]
    lbb = lb[:, None, None, :].astype(f32)
    f = lbb + (1 - lbb) * jax.nn.sigmoid(f_raw)
    log_f = jnp.log(f)
    k = 1 - f

    def to_chunks(z):
        z = jnp.stack([z[0], jnp.flip(z[1], axis=1)])
        z = z.reshape(2, B, NC, C, H, K)
        return jnp.transpose(z, (2, 0, 1, 4, 3, 5))

    def both(z):
        return to_chunks(jnp.broadcast_to(z, (2,) + z.shape))

    mask = jnp.tril(jnp.ones((C, C), dtype=bool))

    def step(S, inp):
        q_c, k_c, v_c, g_c = inp
        G = jnp.cumsum(g_c, axis=-2)
        rel = jnp.where(mask[:, :, None],
                        jnp.exp(jnp.minimum(G[..., :, None, :] - G[..., None, :, :], 0.0)), 0.0)
        A = jnp.einsum('...tk,...sk,...tsk->...ts', q_c, k_c, rel)
        o = jnp.einsum('...ts,...sv->...tv', A, v_c) + jnp.einsum('...tk,...kv->...tv', q_c * jnp.exp(G), S)
        G_last = G[..., -1:, :]
        S = jnp.exp(G_last[..., 0, :])[..., None] * S + \
            jnp.einsum('...sk,...sv->...kv', k_c * jnp.exp(G_last - G), v_c)
        return S, o

    S0 = jnp.zeros((2, B, H, K, K), f32)
    _, o = lax.scan(step, S0, (both(q), to_chunks(k), both(i_in), to_chunks(log_f)))
    o = jnp.transpose(o, (1, 2, 0, 4, 3, 5)).reshape(2, B, T, H, K)
    o = o[0] + jnp.flip(o[1], axis=1)
    o = o * lax.rsqrt(jnp.mean(o * o, axis=-1, keepdims=True) + HGRN_NORM_EPS) * gnorm_w.astype(f32)
    o = o.reshape(B, T, D_HGRN) * jax.nn.silu(gate.astype(f32))
    return o.astype(u.dtype)

def _hier_moe(h, wg, bg, we, be, w_gate, w_up, w_down):
    N, D = h.shape
    glog = (h @ wg + bg).astype(jnp.float32)
    gprob = jax.nn.softmax(glog, axis=-1)
    grp = jnp.argmax(glog, axis=-1)
    p_grp = jnp.take_along_axis(gprob, grp[:, None], axis=-1)
    elog = (h @ we + be).astype(jnp.float32).reshape(N, N_GROUPS, EXPERTS_PER_GROUP)
    elog_g = jnp.take_along_axis(elog, grp[:, None, None], axis=1)[:, 0]
    top_v, top_i = lax.top_k(elog_g, TOP_K_IN_GROUP)
    gate = p_grp * jax.nn.softmax(top_v, axis=-1)
    eid = grp[:, None] * EXPERTS_PER_GROUP + top_i

    M = N * TOP_K_IN_GROUP
    eid_f = eid.reshape(M)
    tok = jnp.repeat(jnp.arange(N), TOP_K_IN_GROUP)
    gate_f = gate.reshape(M)
    order = jnp.argsort(eid_f)
    e_sorted = eid_f[order]
    tok_sorted = tok[order]
    gate_sorted = gate_f[order]
    counts = jnp.bincount(eid_f, length=N_EXPERTS)
    starts = jnp.cumsum(counts) - counts
    padded = (counts + MOE_BLOCK - 1) // MOE_BLOCK * MOE_BLOCK
    pad_ends = jnp.cumsum(padded)
    pad_starts = pad_ends - padded
    dest = pad_starts[e_sorted] + (jnp.arange(M) - starts[e_sorted])
    n_blocks = (M + N_EXPERTS * (MOE_BLOCK - 1) + MOE_BLOCK - 1) // MOE_BLOCK
    P = n_blocks * MOE_BLOCK
    xbuf = jnp.zeros((P, D), h.dtype).at[dest].set(h[tok_sorted])
    block_e = jnp.minimum(jnp.sum(pad_ends[None, :] <= (jnp.arange(n_blocks) * MOE_BLOCK)[:, None], axis=1),
                          N_EXPERTS - 1)

    def run_block(args):
        xb, e = args
        hid = jax.nn.silu(xb @ w_gate[e]) * (xb @ w_up[e])
        return hid @ w_down[e]

    ybuf = lax.map(run_block, (xbuf.reshape(n_blocks, MOE_BLOCK, D), block_e)).reshape(P, D)
    contrib = ybuf[dest] * gate_sorted[:, None].astype(h.dtype)
    return jax.ops.segment_sum(contrib, tok_sorted, num_segments=N)

def _forward(x, norm1_w, w_in, mu_shift, rwkv_w0, rwkv_w2, rwkv_a0, rwkv_a2, rwkv_g2, rwkv_k_k, rwkv_k_a,
             rwkv_r_k, rwkv_lnx_w, rwkv_lnx_b, hgrn_lb, hgrn_gnorm_w, w_out, norm2_w, router_group_w,
             router_group_b, router_expert_w, router_expert_b, moe_w_gate, moe_w_up, moe_w_down, final_norm_w):
    B, T, D = x.shape
    lb_all = jnp.cumsum(jax.nn.softmax(hgrn_lb.astype(jnp.float32), axis=1), axis=1)
    for i in range(DEPTH):
        h = _rms_norm(x, norm1_w[i])
        u = jnp.einsum('btd,dc->btc', h, w_in[i])
        u_r = u[..., :C_RWKV_END]
        u_r = u_r + (_centred_shift(u_r) - u_r) * mu_shift[i]
        y_a = _rwkv7_mixer(u_r, rwkv_w0[i], rwkv_w2[i], rwkv_a0[i], rwkv_a2[i], rwkv_g2[i], rwkv_k_k[i],
                           rwkv_k_a[i], rwkv_r_k[i], rwkv_lnx_w[i], rwkv_lnx_b[i])
        y_b = _hgrn2_mixer(u, lb_all[:, i], hgrn_gnorm_w[i])
        x = x + jnp.einsum('btc,cd->btd', jnp.concatenate([y_a, y_b], axis=-1), w_out[i])
        h2 = _rms_norm(x, norm2_w[i]).reshape(B * T, D)
        x = x + _hier_moe(h2, router_group_w[i], router_group_b[i], router_expert_w[i], router_expert_b[i],
                          moe_w_gate[i], moe_w_up[i], moe_w_down[i]).reshape(B, T, D)
    return _rms_norm(x, final_norm_w)

def setup_inputs(seed: int = 0) -> dict:
    key = jax.random.key(seed)
    ks = jax.random.split(key, 32)
    f32 = jnp.float32
    nrm = lambda k, s, sc: jax.random.normal(k, s, f32) * sc
    L = DEPTH
    return {
        "x_prompt": nrm(ks[0], (BATCH, SEQ, D_MODEL), 1.0),
        "x_sample": nrm(ks[1], (DEC_BATCH, DEC_SEQ, D_MODEL), 1.0),
        "norm1_w": 1.0 + nrm(ks[2], (L, D_MODEL), 0.02),
        "w_in": nrm(ks[3], (L, D_MODEL, D_IN), D_MODEL ** -0.5),
        "mu_shift": jax.random.uniform(ks[4], (L, C_RWKV_END), f32),
        "rwkv_w0": jax.random.uniform(ks[5], (L, 2, D_RWKV), f32, -6.0, -1.0),
        "rwkv_w2": nrm(ks[6], (L, 2, DECAY_LORA, D_RWKV), 0.1),
        "rwkv_a0": nrm(ks[7], (L, 2, D_RWKV), 0.1),
        "rwkv_a2": nrm(ks[8], (L, 2, AAA_LORA, D_RWKV), 0.5 * AAA_LORA ** -0.5),
        "rwkv_g2": nrm(ks[9], (L, GATE_LORA, D_RWKV), GATE_LORA ** -0.5),
        "rwkv_k_k": 0.85 + nrm(ks[10], (L, D_RWKV), 0.02),
        "rwkv_k_a": 1.0 + nrm(ks[11], (L, D_RWKV), 0.02),
        "rwkv_r_k": nrm(ks[12], (L, RWKV_HEADS, RWKV_HEAD), 0.1),
        "rwkv_lnx_w": 1.0 + nrm(ks[13], (L, D_RWKV), 0.02),
        "rwkv_lnx_b": nrm(ks[14], (L, D_RWKV), 0.01),
        "hgrn_lb": nrm(ks[15], (2, L + 1, D_HGRN), 0.5),
        "hgrn_gnorm_w": 1.0 + nrm(ks[16], (L, HGRN_HEAD), 0.02),
        "w_out": nrm(ks[17], (L, D_MIX, D_MODEL), D_MIX ** -0.5),
        "norm2_w": 1.0 + nrm(ks[18], (L, D_MODEL), 0.02),
        "router_group_w": nrm(ks[19], (L, D_MODEL, N_GROUPS), D_MODEL ** -0.5),
        "router_group_b": nrm(ks[20], (L, N_GROUPS), 0.01),
        "router_expert_w": nrm(ks[21], (L, D_MODEL, N_EXPERTS), D_MODEL ** -0.5),
        "router_expert_b": nrm(ks[22], (L, N_EXPERTS), 0.01),
        "moe_w_gate": nrm(ks[23], (L, N_EXPERTS, D_MODEL, D_EXPERT), D_MODEL ** -0.5),
        "moe_w_up": nrm(ks[24], (L, N_EXPERTS, D_MODEL, D_EXPERT), D_MODEL ** -0.5),
        "moe_w_down": nrm(ks[25], (L, N_EXPERTS, D_EXPERT, D_MODEL), D_EXPERT ** -0.5),
        "final_norm_w": 1.0 + nrm(ks[26], (D_MODEL,), 0.02),
    }

def reference(x_prompt, x_sample, norm1_w, w_in, mu_shift, rwkv_w0, rwkv_w2, rwkv_a0, rwkv_a2, rwkv_g2,
              rwkv_k_k, rwkv_k_a, rwkv_r_k, rwkv_lnx_w, rwkv_lnx_b, hgrn_lb, hgrn_gnorm_w, w_out, norm2_w,
              router_group_w, router_group_b, router_expert_w, router_expert_b, moe_w_gate, moe_w_up,
              moe_w_down, final_norm_w):
    weights = (norm1_w, w_in, mu_shift, rwkv_w0, rwkv_w2, rwkv_a0, rwkv_a2, rwkv_g2, rwkv_k_k, rwkv_k_a,
               rwkv_r_k, rwkv_lnx_w, rwkv_lnx_b, hgrn_lb, hgrn_gnorm_w, w_out, norm2_w, router_group_w,
               router_group_b, router_expert_w, router_expert_b, moe_w_gate, moe_w_up, moe_w_down, final_norm_w)
    y_prompt = _forward(x_prompt, *weights)
    y_sample = _forward(x_sample, *weights)
    return (y_prompt, y_sample)


_drawn_inputs = setup_inputs


def setup_inputs(seed=0):
    import zlib

    import numpy as np

    out = dict(_drawn_inputs(seed))
    spreads = {}
    factors = {'rwkv_k_k': 9.09,
     'rwkv_k_a': 2.839,
     'rwkv_lnx_w': 10.09,
     'rwkv_lnx_b': 16.761,
     'hgrn_gnorm_w': 8.307,
     'router_group_b': 21.71,
     'router_expert_b': 14.816,
     'final_norm_w': 7.842,
     'norm2_w': 3.215}
    for name, (base, spread) in spreads.items():
        noise = np.random.default_rng([zlib.crc32(name.encode()), seed]).standard_normal(out[name].shape)
        drawn = base * np.exp(spread * noise) if base else spread * noise
        out[name] = __import__('jax').numpy.asarray(drawn.astype(out[name].dtype))
    for name, factor in factors.items():
        out[name] = (out[name] * factor).astype(out[name].dtype)
    return out
```

```python
from contextlib import ExitStack

import numpy as np
import concourse.bass as bass
from concourse import mybir

F32 = mybir.dt.float32
I32 = mybir.dt.int32
U32 = mybir.dt.uint32
ALU = mybir.AluOpType
ACT = mybir.ActivationFunctionType
AX_X = mybir.AxisListType.X

P = 128
D = 1024
KT = D // P
SEQ_P, SEQ_S = 1024, 512
T = SEQ_P + SEQ_S
SPAN = 512
SPANS = T // SPAN
TILES = T // P
CH = 32
CHUNKS = T // CH
DR = 512
RH = 64
PAIRS = DR // P
CW = SPAN // CH
C_R, C_K, C_V, C_WD = 0, DR, 2 * DR, 3 * DR
C_AD, C_GD, C_Q = C_WD + 128, C_WD + 256, C_WD + 384
C_F, C_I = C_Q + DR, C_Q + 3 * DR
C_G = C_I + DR
DECAY = float(np.exp(-0.5))
NG, EG, NE, DE = 4, 8, 32, 512
KD = DE // P
NBLK = 2 * T // P + NE - 1
NBLK += NBLK % 2
NSLOT = NBLK + 3
SEGMENTS = ((0, SEQ_P // P), (SEQ_P // P, SEQ_S // P))


SPANS_P = SEQ_P // SPAN


def slot(d, s):
    return s if d == 0 or s >= SPANS_P else SPANS_P - 1 - s


def step_of(c):
    last = SEQ_P // CH - 1
    return last - c if c <= last else last + CHUNKS - c


WAY = (slice(None), slice(None, None, -1))


class Marks:

    def __init__(self, sem, names, base=0):
        self.sem, self.names, self.base, self.k = sem, names.split(), base, 0

    def inc(self, name):
        assert self.names[self.k] == name, (self.names[self.k], name)
        self.k = (self.k + 1) % len(self.names)
        return self.sem, 1

    def ago(self, name, step, back):
        return None if isinstance(step, int) and step < back else self.at(name, step - back)

    def at(self, name, step):
        return self.sem, step * len(self.names) + (self.base + self.names.index(name) + 1)


class Kernel:
    def __init__(self, nc, args, outs, upto):
        self.nc, self.a, self.outs, self.upto = nc, args, outs, upto
        self.ctx = ExitStack()

    def sem(self, name):
        return self.ctx.enter_context(self.nc.semaphore(name))

    def dram(self, name, shape, dt=F32):
        return self.nc.dram_tensor(name, shape, dt, kind="Internal").ap()

    def build(self):
        nc = self.nc
        with self.ctx:
            self.keep = self.ctx
            sb = lambda n, s, dt=F32: self.ctx.enter_context(nc.sbuf_tensor(n, s, dt))
            self.ident = sb("ident", [P, P])
            self.headsum = sb("headsum", [P, P])
            self.allsum = sb("allsum", [P, P])
            self.sp_turn = self.sem("sp_turn")
            self.pe_turn = self.sem("pe_turn")
            self.pool_turn = self.sem("pool_turn")
            self.kb = self.dram("kb", (2, PAIRS, P, CHUNKS, 2 * CH))
            self.ar = self.dram("ar", (2, PAIRS, P, CHUNKS, 2 * CH))
            self.kq = self.dram("kq", (2, PAIRS, 2, P, T))
            self.vtok = self.dram("vtok", (2, T, DR))
            self.itok = self.dram("itok", (2, T, DR))
            self.bonusv = self.dram("bonusv", (PAIRS, P, T))
            self.rgate = self.dram("rgate", (PAIRS, P, T))
            self.hgate = self.dram("hgate", (PAIRS, P, T))
            self.rdecay = self.dram("rdecay", (2, PAIRS, P, CHUNKS))
            self.hdecay = self.dram("hdecay", (2, PAIRS, P, CHUNKS))
            self.yT = self.dram("yT", (2, 2 * PAIRS, P, T))
            self.x1 = self.dram("x1", (T, D))
            self.h2 = self.dram("h2", (T, D))
            self.slots = self.dram("slots", (NSLOT * P, 2), U32)
            self.ytok = self.dram("ytok", (2 * T + P, D))
            self.constants()
            with ExitStack() as hctx:
                self.hT = hctx.enter_context(nc.sbuf_tensor("hT", [P, KT, T], F32))
                if self.upto >= 1:
                    self.norm_in()
                if self.upto >= 2:
                    self.project_rwkv()
                if self.upto >= 3:
                    self.project_hgrn()
            if self.upto >= 4:
                self.mix_rwkv()
            if self.upto >= 5:
                self.mix_hgrn()
            self.logits = sb("logits", [P, TILES, NG + NE])
            if self.upto >= 6:
                self.mixer_out()
            self.gate = [sb(f"gate{k}", [P, TILES]) for k in range(2)]
            self.expert = sb("expert", [P, NBLK], I32)
            self.rounds = sb("rounds", [P, 1], I32)
            with ExitStack() as ectx:
                wsb = lambda n, s: ectx.enter_context(nc.sbuf_tensor("e_" + n, s, F32))
                self.wg, self.wu = ([wsb(f"{n}{u}", [P, KT, DE]) for u in range(2)] for n in ("wg", "wu"))
                self.wd = [wsb(f"wd{u}", [P, KD, D]) for u in range(2)]
                self.w_loaded = [self.sem(f"e_w_loaded{u}") for u in range(2)]
                if self.upto >= 7:
                    self.route()
                if self.upto >= 8:
                    self.experts()
            if self.upto >= 9:
                self.combine()

    def waits(self, eng, *waits):
        for w in waits:
            if w is not None:
                eng.wait_ge(*w)

    def hold_sp(self, sp, *waits):
        self.waits(sp, *waits)
        sp.sem_inc(self.sp_turn, 1)

    def hold_pe(self, pe, *waits):
        self.waits(pe, *waits)
        pe.sem_inc(self.pe_turn, 1)

    def store_tokens(self, eng, dst, src, s, cols, sem):
        t0 = s * SPAN
        tiles = src[:].rearrange("p (i n) -> p i n", n=P)
        eng.dma_start(dst[0, t0:t0 + SPAN, cols].rearrange("(i p) n -> p i n", p=P), tiles).then_inc(sem, 16)
        by_step = dst[1, :, cols].rearrange("(c k) n -> k c n", k=CH)
        for q in range(P // CH):
            first = step_of(s * CW + q)
            rows = by_step[:, first - (CW - P // CH):first + 1:P // CH][:, ::-1]
            eng.dma_start(rows, tiles[q * CH:(q + 1) * CH]).then_inc(sem, 16)

    def constants(self):
        nc = self.nc
        made = self.sem("const_made")
        with nc.Block() as block:
            @block.gpsimd
            def _(pool):
                nc.gpsimd.memset(self.ident[:], 0.0).then_inc(made, 1)
                nc.gpsimd.memset(self.headsum[:], 1.0).then_inc(made, 1)
                nc.gpsimd.memset(self.allsum[:], 1.0).then_inc(made, 1)
                pool.wait_ge(made, 3)
                nc.gpsimd.affine_select(out=self.ident[:], in_=self.ident[:], compare_op=ALU.not_equal, fill=1.0,
                                        base=0, pattern=[[-1, P]], channel_multiplier=1).then_inc(made, 1)
                nc.gpsimd.affine_select(out=self.headsum[:, 0:RH], in_=self.headsum[:, 0:RH], compare_op=ALU.is_gt,
                                        fill=0.0, base=RH, pattern=[[0, RH]], channel_multiplier=-1).then_inc(made, 1)
                nc.gpsimd.affine_select(out=self.headsum[:, RH:], in_=self.headsum[:, RH:], compare_op=ALU.is_ge,
                                        fill=0.0, base=-RH, pattern=[[0, RH]], channel_multiplier=1).then_inc(made, 1)
                pool.wait_ge(made, 6)

    def norm_in(self):
        nc = self.nc
        with ExitStack() as ctx:
            sb = lambda n, s, dt=F32: ctx.enter_context(nc.sbuf_tensor(n, s, dt))
            x = sb("n_x", [P, 2, D])
            xs = sb("n_xs", [P, 2, D])
            junk = sb("n_junk", [P, 2, D])
            ss = sb("n_ss", [P, 2])
            rt = sb("n_rt", [P, 2])
            rs = sb("n_rs", [P, 2])
            w = sb("n_w", [P, KT])
            pt = [ctx.enter_context(nc.psum_tensor(f"n_pt{u}", [P, D], F32)) for u in range(2)]
            x_loaded = [self.sem(f"n_x_loaded{u}") for u in range(2)]
            w_loaded = self.sem("n_w_loaded")
            act = Marks(self.sem("n_act_done"), "squares root")
            dve = Marks(self.sem("n_dve_done"), "meansq inverse scaled turned")
            pe = Marks(self.sem("n_pe_done"), "transposed")
            eps = 1e-6

            def tiles(eng, body):
                for (t0, n), src in zip(SEGMENTS, (self.a["x_prompt"], self.a["x_sample"])):
                    with eng.Fori(0, n // 2) as half:
                        for u in range(2):
                            body(src[0], half * 2 + u, half * 2 + (t0 + u), u, half + t0 // 2)

            with nc.Block() as block:
                @block.sync
                def _(sp):
                    sp.sem_inc(dve.sem, 2 * 4)
                    with nc.allow_non_contiguous_dma(reason="a small weight, channel-major"):
                        sp.dma_start(w[:], self.a["norm1_w"][0].rearrange("(c p) -> p c", p=P)).then_inc(w_loaded, 16)

                    def load(src, k, t, u, turn):
                        self.hold_sp(sp, dve.at("scaled", t))
                        sp.dma_start(x[:, u], src[bass.ds(k * P, P), :]).then_inc(x_loaded[u], 16)
                    tiles(sp, load)

                @block.scalar
                def _(eng):
                    def squares(src, k, t, u, turn):
                        eng.wait_ge(x_loaded[u], turn * 16 + 16)
                        eng.wait_ge(*dve.at("meansq", t))
                        nc.scalar.activation(junk[:, u], x[:, u], ACT.Square,
                                             accum_out=ss[:, u:u + 1]).then_inc(*act.inc("squares"))
                        eng.wait_ge(*dve.at("meansq", t + 2))
                        nc.scalar.activation(rt[:, u:u + 1], rs[:, u:u + 1], ACT.Sqrt).then_inc(*act.inc("root"))
                    tiles(eng, squares)

                @block.vector
                def _(eng):
                    eng.wait_ge(w_loaded, 16)

                    def scale(src, k, t, u, turn):
                        eng.wait_ge(*act.at("squares", t))
                        nc.vector.tensor_scalar(rs[:, u:u + 1], ss[:, u:u + 1], 1.0 / D, eps, ALU.mult,
                                                ALU.add).then_inc(*dve.inc("meansq"))
                        eng.wait_ge(*act.at("root", t))
                        nc.vector.reciprocal(rs[:, u:u + 1], rt[:, u:u + 1]).then_inc(*dve.inc("inverse"))
                        eng.wait_ge(*dve.at("inverse", t + 2))
                        nc.vector.tensor_scalar(xs[:, u], x[:, u], rs[:, u:u + 1], None,
                                                ALU.mult).then_inc(*dve.inc("scaled"))
                        eng.wait_ge(*pe.at("transposed", t))
                        nc.vector.tensor_tensor(self.hT[:, :, bass.ds(t * P, P)],
                                                pt[u][:].rearrange("p (c k) -> p c k", c=KT),
                                                w[:].unsqueeze(2).broadcast_to((P, KT, P)),
                                                ALU.mult).then_inc(*dve.inc("turned"))
                    tiles(eng, scale)

                @block.tensor
                def _(eng):
                    def transposes(src, k, t, u, turn):
                        self.hold_pe(eng, dve.at("scaled", t + 2), dve.at("turned", t))
                        for c in range(KT):
                            last = nc.tensor.transpose(pt[u][:, c * P:(c + 1) * P], xs[:, u, c * P:(c + 1) * P],
                                                       self.ident[:])
                        last.then_inc(*pe.inc("transposed"))
                    tiles(eng, transposes)

    def project_rwkv(self):
        nc = self.nc
        a = self.a
        PAD = T + 4
        at = [s * SPAN if s < SEQ_P // SPAN else s * SPAN + 2 for s in range(SPANS)]
        W = T + 2
        with ExitStack() as ctx:
            sb = lambda n, s, dt=F32: ctx.enter_context(nc.sbuf_tensor(n, s, dt))
            psum = lambda n: ctx.enter_context(nc.psum_tensor(n, [P, SPAN], F32))
            wcol = [sb(f"r_wcol{q}", [P, KT, P]) for q in range(3)]
            raw = [sb(f"r_raw{q}", [P, PAD]) for q in range(3)]
            mixed = [[sb(f"r_mix{u}{q}", [P, W]) for q in range(3)] for u in range(2)]
            nbr = sb("r_nbr", [P, W])
            tanh_w, low_a, sig_g = (sb(n, [P, W]) for n in ("r_tanhw", "r_lowa", "r_sigg"))
            low = [[sb(f"r_low{u}{n}", [P, P]) for n in "wag"] for u in range(2)]
            kk = sb("r_kk", [P, T])
            ksq = sb("r_ksq", [P, SPAN])
            restart = sb("r_restart", [P, SPAN])
            sg, av, gi, gx, kd, bv = ([sb(f"r_{n}_{d}", [P, SPAN]) for d in range(2)]
                                      for n in ("sg", "a", "gi", "gx", "kd", "b"))
            e_in, e_out, e_prev = (sb(n, [P, SPAN]) for n in ("r_e_in", "r_e_out", "r_e_prev"))
            ksum = sb("r_ksum", [P, SPAN])
            kbst = [sb(f"r_kb{d}", [P, CW, 2 * CH]) for d in range(2)]
            arst = [sb(f"r_ar{d}", [P, CW, 2 * CH]) for d in range(2)]
            dcst = sb("r_dc", [P, 2, CW])
            gst, vst, bst = (sb(n, [P, SPAN]) for n in ("r_gst", "r_vst", "r_bst"))
            mu, hmu, omu = (sb(n, [P, 15]) for n in ("r_mu", "r_hmu", "r_omu"))
            w0, a0 = sb("r_w0", [P, 2, PAIRS]), sb("r_a0", [P, 2, PAIRS])
            k_k, k_a, oka, r_k = (sb(n, [P, PAIRS]) for n in ("r_kkw", "r_kaw", "r_oka", "r_rk"))
            pp = [psum(f"r_pp{s}") for s in range(3)]
            pl = [psum(f"r_pl{s}") for s in range(2)]
            pg, pv, pn = psum("r_pg"), psum("r_pv"), psum("r_pn")

            consts = self.sem("r_consts")
            params = self.sem("r_params")
            setup = self.sem("r_setup")
            cleared = self.sem("r_cleared")
            w_loaded = [self.sem(f"r_w_loaded{q}") for q in range(3)]
            low_loaded = [self.sem(f"r_low_loaded{u}") for u in range(2)]
            stored = {n: self.sem("r_stored_" + n) for n in ("kb0", "kb1", "ar0", "ar1", "dc", "g", "v", "b")}
            pe_proj = Marks(self.sem("r_pe_proj"), "p0 p1 p2 p3 p4 p5 p6 p7 p8")
            act_ev = Marks(self.sem("r_act_ev"), "e0 e1 e2 e3 e4 e5 e6 e7 e8")
            dve_mix = Marks(self.sem("r_dve_mix"), "keep0 nbr0 mixed0 keep1 nbr1 mixed1 keep2 nbr2 mixed2")
            act_low = self.sem("r_act_low")
            act_norm = Marks(self.sem("r_act_norm"), "sq0 sq1 sq2 root0 root1 root2")
            pe_norm = Marks(self.sem("r_pe_norm"), "ss0 ss1 ss2")
            dve_norm = Marks(self.sem("r_dve_norm"), "max0 max1 max2 inv0 kk0 inv1 kk1 inv2 kk2")
            pe_aux = Marks(self.sem("r_pe_aux"), "W0 A0 W1 A1 G V BONUS")
            act_aux = Marks(self.sem("r_act_aux"),
                            "sg0 a0 sg1 a1 g v in0 out0 prev0 dc0 in1 out1 prev1 dc1")
            pool_aux = Marks(self.sem("r_pool_aux"), "gx0 gx1 b0 b1")
            dve_aux = Marks(self.sem("r_dve_aux"),
                            "scan0 scan1 kf0 kd0 kf1 kd1 ksum kr R0 A0 K0 B0 R1 A1 K1 B1 bonus")
            GROUPS = PAIRS + 1

            def col(g, q):
                return 12 + q if g == 0 else (g - 1) + (1, 2, 0)[q] * PAIRS

            with nc.Block() as block:
                @block.sync
                def _(sp):
                    with nc.allow_non_contiguous_dma(reason="small weights, channel-major"):
                        for dst, src in ((mu[:], a["mu_shift"][0].rearrange("(t p) -> p t", p=P)),
                                         (k_k[:], a["rwkv_k_k"][0].rearrange("(t p) -> p t", p=P)),
                                         (k_a[:], a["rwkv_k_a"][0].rearrange("(t p) -> p t", p=P)),
                                         (r_k[:], a["rwkv_r_k"][0].rearrange("(t two) k -> (two k) t", two=2)),
                                         (w0[:, 0], a["rwkv_w0"][0, 0].rearrange("(t p) -> p t", p=P)),
                                         (w0[:, 1], a["rwkv_w0"][0, 1].rearrange("(t p) -> p t", p=P)),
                                         (a0[:, 0], a["rwkv_a0"][0, 0].rearrange("(t p) -> p t", p=P)),
                                         (a0[:, 1], a["rwkv_a0"][0, 1].rearrange("(t p) -> p t", p=P))):
                            sp.dma_start(dst, src).then_inc(params, 16)

                    def load_w(g, q):
                        c = col(g, q) * P
                        if g:
                            self.hold_sp(sp, pe_proj.at(f"p{3 * q + 2}", g - 1))
                        sp.dma_start(wcol[q][:], a["w_in"][0, :, c:c + P].rearrange("(k p) n -> p k n", p=P)
                                     ).then_inc(w_loaded[q], 16)

                    def load_low(j, u, guard):
                        if guard:
                            self.hold_sp(sp, pe_aux.at("G", 3 * j - 4))
                        c = j * P
                        for i, (dst, src) in enumerate((
                                (low[u][0][:], a["rwkv_w2"][0, :, :, c:c + P].rearrange("d r n -> (d r) n")),
                                (low[u][1][:], a["rwkv_a2"][0, :, :, c:c + P].rearrange("d r n -> (d r) n")),
                                (low[u][2][:], a["rwkv_g2"][0, :, c:c + P]))):
                            sp.dma_start(dst, src).then_inc(low_loaded[u], 16)

                    def store(j, s):
                        n = 3 * j + s
                        t0 = s * SPAN
                        for d in range(2):
                            self.hold_sp(sp, dve_aux.at(f"A{d}", n))
                            sp.dma_start(self.ar[d, j:j + 1, :, slot(d, s) * CW:(slot(d, s) + 1) * CW].rearrange(
                                "o p c k -> p (o c) k"), arst[d][:]).then_inc(stored[f"ar{d}"], 16)
                            self.hold_sp(sp, dve_aux.at(f"B{d}", n))
                            sp.dma_start(self.kb[d, j:j + 1, :, slot(d, s) * CW:(slot(d, s) + 1) * CW].rearrange(
                                "o p c k -> p (o c) k"), kbst[d][:]).then_inc(stored[f"kb{d}"], 16)
                        self.hold_sp(sp, act_aux.at("dc1", n))
                        for d in range(2):
                            c0 = slot(d, s) * CW
                            sp.dma_start(self.rdecay[d, j, :, c0:c0 + CW], dcst[:, d]).then_inc(stored["dc"], 16)
                        sp.dma_start(self.rgate[j:j + 1, :, t0:t0 + SPAN].rearrange("o p t -> p (o t)"),
                                     gst[:]).then_inc(stored["g"], 16)
                        self.store_tokens(sp, self.vtok, vst, s, slice(j * P, (j + 1) * P), stored["v"])
                        self.hold_sp(sp, dve_aux.at("bonus", n))
                        sp.dma_start(self.bonusv[j:j + 1, :, t0:t0 + SPAN].rearrange("o p t -> p (o t)"),
                                     bst[:]).then_inc(stored["b"], 16)

                    for q in range(3):
                        load_w(0, q)
                    load_low(0, 0, False)
                    load_low(1, 1, False)
                    for q in range(3):
                        load_w(1, q)

                    for j in range(PAIRS):
                        for s in range(SPANS):
                            if j + 2 <= PAIRS:
                                load_w(j + 2, s)
                            store(j, s)
                        if j + 2 < PAIRS:
                            load_low(j + 2, j % 2, True)
                    for name, s in stored.items():
                        sp.wait_ge(s, 16 * 3 * PAIRS * {"v": 5, "dc": 2}.get(name, 1))

                @block.tensor
                def _(eng):
                    def proj(g, q):
                        for s in range(SPANS):
                            k = 3 * q + s
                            waits = [(w_loaded[q], g * 16 + 16)] if s == 0 else []
                            if k >= 3:
                                waits.append(act_ev.at(f"e{k - 3}", g))
                            elif g:
                                waits.append(act_ev.at(f"e{k + 6}", g - 1))
                            if waits:
                                self.hold_pe(eng, *waits)
                            for c in range(KT):
                                last = nc.tensor.matmul(pp[s][:], wcol[q][:, c], self.hT[:, c, s * SPAN:(s + 1) * SPAN],
                                                        start=c == 0, stop=c == KT - 1)
                            last.then_inc(*pe_proj.inc(f"p{k}"))

                    def norm(j):
                        for s in range(SPANS):
                            waits = [act_norm.at(f"sq{s}", j)]
                            if s:
                                waits.append(dve_norm.at(f"max{s - 1}", j))
                            self.hold_pe(eng, *waits)
                            nc.tensor.matmul(pn[:], self.headsum[:], ksq[:], start=True, stop=True
                                             ).then_inc(*pe_norm.inc(f"ss{s}"))

                    def aux_a(j, s, u):
                        n = 3 * j + s
                        t = slice(at[s], at[s] + SPAN)
                        if s == 0:
                            self.hold_pe(eng, (low_loaded[u], (j - u) * 24 + 48))
                        for d in range(2):
                            r = slice(64 * d, 64 * d + 64)
                            self.hold_pe(eng, act_aux.at("sg0", n) if d else act_aux.at("sg1", n - 1) if n else
                                         (act_low, 3))
                            nc.tensor.matmul(pl[0][:], low[u][0][r, :], tanh_w[r, t], start=True, stop=True
                                             ).then_inc(*pe_aux.inc(f"W{d}"))
                            if n or d:
                                self.hold_pe(eng, act_aux.at("a0", n) if d else act_aux.at("a1", n - 1))
                            nc.tensor.matmul(pl[1][:], low[u][1][r, :], low_a[r, t], start=True, stop=True
                                             ).then_inc(*pe_aux.inc(f"A{d}"))
                        if n:
                            self.hold_pe(eng, dve_aux.at("bonus", n - 1), act_aux.at("v", n - 1))
                        nc.tensor.matmul(pg[:], low[u][2][:], sig_g[:, t], start=True, stop=True
                                         ).then_inc(*pe_aux.inc("G"))
                        if s == 0:
                            self.hold_pe(eng, dve_mix.at("mixed1", j + 1))
                        for i in range(SPAN // P):
                            last = nc.tensor.transpose(pv[:, i * P:(i + 1) * P],
                                                       mixed[1 - u][1][:, at[s] + i * P:at[s] + (i + 1) * P],
                                                       self.ident[:])
                        last.then_inc(*pe_aux.inc("V"))

                    def aux_b(j, s):
                        n = 3 * j + s
                        self.hold_pe(eng, dve_aux.at("kr", n), act_aux.at("g", n))
                        nc.tensor.matmul(pg[:], self.headsum[:], ksum[:], start=True, stop=True
                                         ).then_inc(*pe_aux.inc("BONUS"))

                    def first():
                        for q in range(3):
                            proj(0, q)
                        for q in range(3):
                            proj(1, q)
                        norm(0)

                    first()
                    for j in range(PAIRS):
                        for s in range(SPANS):
                            aux_a(j, s, j % 2)
                            if j + 2 <= PAIRS:
                                proj(j + 2, s)
                            aux_b(j, s)
                        if j + 1 < PAIRS:
                            norm(j + 1)

                @block.scalar
                def _(eng):
                    def evac(g, q):
                        for s in range(SPANS):
                            k = 3 * q + s
                            eng.wait_ge(*pe_proj.at(f"p{k}", g))
                            if s == 0 and g:
                                eng.wait_ge(*dve_mix.at(f"mixed{q}", g - 1))
                            nc.scalar.activation(raw[q][:, at[s] + 1:at[s] + 1 + SPAN], pp[s][:], ACT.Copy
                                                 ).then_inc(*act_ev.inc(f"e{k}"))

                    def norm_sq(j, u):
                        for s in range(SPANS):
                            if s == 0:
                                eng.wait_ge(*dve_mix.at("mixed0", j + 1))
                            else:
                                eng.wait_ge(*pe_norm.at(f"ss{s - 1}", j))
                            nc.scalar.activation(ksq[:], mixed[u][0][:, at[s]:at[s] + SPAN], ACT.Square,
                                                 scale=k_k[:, j:j + 1]).then_inc(*act_norm.inc(f"sq{s}"))

                    def norm_root(j):
                        for s in range(SPANS):
                            eng.wait_ge(*dve_norm.at(f"max{s}", j))
                            t = slice(s * SPAN, (s + 1) * SPAN)
                            nc.scalar.activation(kk[:, t], kk[:, t], ACT.Sqrt).then_inc(*act_norm.inc(f"root{s}"))

                    def aux(j, s, zero):
                        n = 3 * j + s
                        for d in range(2):
                            eng.wait_ge(*pe_aux.at(f"W{d}", n))
                            if not zero:
                                eng.wait_ge(*pool_aux.at(f"gx{d}", n - 1))
                            nc.scalar.activation(sg[d][:], pl[0][:], ACT.Sigmoid, bias=w0[:, d, j:j + 1]
                                                 ).then_inc(*act_aux.inc(f"sg{d}"))
                            eng.wait_ge(*pe_aux.at(f"A{d}", n))
                            if not zero:
                                eng.wait_ge(*pool_aux.at(f"b{d}", n - 1))
                                eng.wait_ge(*dve_aux.at(f"kf{d}", n - 1))
                            nc.scalar.activation(av[d][:], pl[1][:], ACT.Sigmoid, bias=a0[:, d, j:j + 1]
                                                 ).then_inc(*act_aux.inc(f"a{d}"))
                        eng.wait_ge(*pe_aux.at("G", n))
                        eng.wait_ge(stored["g"], n * 16)
                        nc.scalar.activation(gst[:], pg[:], ACT.Copy).then_inc(*act_aux.inc("g"))
                        eng.wait_ge(*pe_aux.at("V", n))
                        eng.wait_ge(stored["v"], n * 16 * 5)
                        nc.scalar.activation(vst[:], pv[:], ACT.Copy).then_inc(*act_aux.inc("v"))
                        for d in range(2):
                            eng.wait_ge(*dve_aux.at(f"scan{d}", n))
                            if d:
                                eng.wait_ge(*dve_aux.at("R0", n))
                            elif not zero:
                                eng.wait_ge(*dve_aux.at("B1", n - 1))
                            nc.scalar.activation(e_in[:], gi[d][:], ACT.Exp, scale=-DECAY
                                                 ).then_inc(*act_aux.inc(f"in{d}"))
                            if d:
                                eng.wait_ge(*dve_aux.at("B0", n))
                            nc.scalar.activation(e_out[:], gi[d][:], ACT.Exp, scale=DECAY
                                                 ).then_inc(*act_aux.inc(f"out{d}"))
                            eng.wait_ge(*pool_aux.at(f"gx{d}", n))
                            nc.scalar.activation(e_prev[:], gx[d][:], ACT.Exp, scale=-DECAY
                                                 ).then_inc(*act_aux.inc(f"prev{d}"))
                            if d == 0:
                                eng.wait_ge(stored["dc"], n * 16 * 2)
                            edge = gi[d][:].rearrange("p (c k) -> p c k", k=CH)[:, :, (CH - 1, 0)[d]:(CH, 1)[d]]
                            nc.scalar.activation(dcst[:, d, WAY[d]].unsqueeze(2), edge, ACT.Exp, scale=-DECAY
                                                 ).then_inc(*act_aux.inc(f"dc{d}"))

                    eng.wait_ge(params, 16 * 8)
                    eng.wait_ge(cleared, 5)
                    eng.wait_ge(setup, 3)
                    for q in range(3):
                        evac(0, q)
                    for q, (dst, f) in enumerate(((tanh_w, ACT.Tanh), (low_a, ACT.Copy), (sig_g, ACT.Sigmoid))):
                        eng.wait_ge(*dve_mix.at(f"mixed{q}", 0))
                        nc.scalar.activation(dst[:], mixed[0][q][:], f).then_inc(act_low, 1)
                    for q in range(3):
                        evac(1, q)
                    norm_sq(0, 1)
                    norm_root(0)
                    for j in range(PAIRS):
                        for s in range(SPANS):
                            aux(j, s, 3 * j + s == 0)
                            if j + 2 <= PAIRS:
                                evac(j + 2, s)
                        if j + 1 < PAIRS:
                            norm_sq(j + 1, j % 2)
                            norm_root(j + 1)

                @block.gpsimd
                def _(pool):
                    nc.gpsimd.memset(restart[:], 1.0).then_inc(cleared, 1)
                    pool.wait_ge(cleared, 1)
                    nc.gpsimd.memset(restart[:].rearrange("p (c k) -> p c k", k=CH)[:, :, 0:1], 0.0).then_inc(cleared, 1)
                    for q in range(3):
                        nc.gpsimd.memset(raw[q][:], 0.0).then_inc(cleared, 1)

                    def aux(j, s, zero):
                        n = 3 * j + s
                        for d in range(2):
                            pool.wait_ge(*dve_aux.at(f"scan{d}", n))
                            if not zero:
                                pool.wait_ge(*act_aux.at(f"prev{d}", n - 1))
                            nc.gpsimd.tensor_tensor(gx[d][:], gi[d][:], sg[d][:], ALU.subtract
                                                    ).then_inc(*pool_aux.inc(f"gx{d}"))
                        for d in range(2):
                            if d == 0 and s == 0:
                                pool.wait_ge(*dve_norm.at("kk2", j))
                            pool.wait_ge(*act_aux.at(f"a{d}", n))
                            if not zero:
                                pool.wait_ge(*dve_aux.at(f"B{d}", n - 1))
                            nc.gpsimd.tensor_tensor(bv[d][:], kk[:, s * SPAN:(s + 1) * SPAN], av[d][:], ALU.mult
                                                    ).then_inc(*pool_aux.inc(f"b{d}"))
                    for j in range(PAIRS):
                        for s in range(SPANS):
                            aux(j, s, 3 * j + s == 0)

                @block.vector
                def _(eng):
                    eng.wait_ge(params, 16 * 8)
                    nc.vector.tensor_scalar(hmu[:], mu[:], 0.5, None, ALU.mult).then_inc(setup, 1)
                    nc.vector.tensor_scalar(omu[:], mu[:], -1.0, 1.0, ALU.mult, ALU.add).then_inc(setup, 1)
                    nc.vector.tensor_scalar(oka[:], k_a[:], -1.0, 1.0, ALU.mult, ALU.add).then_inc(setup, 1)
                    eng.wait_ge(setup, 3)
                    eng.wait_ge(cleared, 5)

                    def mix(g, q, u):
                        eng.wait_ge(*act_ev.at(f"e{3 * q + 2}", g))
                        c = slice(col(g, q), col(g, q) + 1)
                        nc.vector.tensor_scalar(mixed[u][q][:], raw[q][:, 1:1 + W], omu[:, c], None, ALU.mult
                                                ).then_inc(*dve_mix.inc(f"keep{q}"))
                        if q:
                            eng.wait_ge(*dve_mix.at(f"mixed{q - 1}", g))
                        elif not (isinstance(g, int) and g == 0):
                            eng.wait_ge(*dve_mix.at("mixed2", g - 1))
                        nc.vector.tensor_tensor(nbr[:], raw[q][:, 0:W], raw[q][:, 2:2 + W], ALU.add
                                                ).then_inc(*dve_mix.inc(f"nbr{q}"))
                        eng.wait_ge(*dve_mix.at(f"nbr{q}", g))
                        nc.vector.scalar_tensor_tensor(mixed[u][q][:], nbr[:], hmu[:, c], mixed[u][q][:], ALU.mult,
                                                       ALU.add).then_inc(*dve_mix.inc(f"mixed{q}"))

                    def norm_max(j):
                        for s in range(SPANS):
                            eng.wait_ge(*pe_norm.at(f"ss{s}", j))
                            nc.vector.tensor_scalar(kk[:, s * SPAN:(s + 1) * SPAN], pn[:], 1e-24, None, ALU.max
                                                    ).then_inc(*dve_norm.inc(f"max{s}"))

                    def norm_kk(j, u):
                        for s in range(SPANS):
                            t = slice(s * SPAN, (s + 1) * SPAN)
                            eng.wait_ge(*act_norm.at(f"root{s}", j))
                            nc.vector.reciprocal(kk[:, t], kk[:, t]).then_inc(*dve_norm.inc(f"inv{s}"))
                            eng.wait_ge(*dve_norm.at(f"inv{s}", j))
                            nc.vector.scalar_tensor_tensor(kk[:, t], mixed[u][0][:, at[s]:at[s] + SPAN],
                                                           k_k[:, j:j + 1], kk[:, t], ALU.mult, ALU.mult
                                                           ).then_inc(*dve_norm.inc(f"kk{s}"))

                    def aux(j, s, u, zero):
                        n = 3 * j + s
                        m = slice(at[s], at[s] + SPAN)
                        c = slice(j, j + 1)
                        mk, mv, mr = (mixed[u][q][:, m] for q in range(3))
                        split = lambda ap: ap.rearrange("p (c k) -> p c k", k=CH)
                        for d in range(2):
                            eng.wait_ge(*act_aux.at(f"sg{d}", n))
                            if not zero:
                                eng.wait_ge(*act_aux.at(f"dc{d}", n - 1))
                                eng.wait_ge(*pool_aux.at(f"gx{d}", n - 1))
                            nc.vector.tensor_tensor_scan(gi[d][:, WAY[d]], restart[:], sg[d][:, WAY[d]], 0.0, ALU.mult,
                                                         ALU.add).then_inc(*dve_aux.inc(f"scan{d}"))
                        for d in range(2):
                            eng.wait_ge(*act_aux.at(f"a{d}", n))
                            nc.vector.tensor_scalar(kd[d][:], av[d][:], k_a[:, c], oka[:, c], ALU.mult, ALU.add
                                                    ).then_inc(*dve_aux.inc(f"kf{d}"))
                            eng.wait_ge(*dve_aux.at(f"kf{d}", n))
                            nc.vector.tensor_tensor(kd[d][:], kd[d][:], mk, ALU.mult).then_inc(*dve_aux.inc(f"kd{d}"))
                        eng.wait_ge(*dve_aux.at("kd1", n))
                        if not zero:
                            eng.wait_ge(*pe_aux.at("BONUS", n - 1))
                        nc.vector.tensor_tensor(ksum[:], kd[0][:], kd[1][:], ALU.add).then_inc(*dve_aux.inc("ksum"))
                        eng.wait_ge(*dve_aux.at("ksum", n))
                        nc.vector.scalar_tensor_tensor(ksum[:], mr, r_k[:, c], ksum[:], ALU.mult, ALU.mult
                                                       ).then_inc(*dve_aux.inc("kr"))
                        for d in range(2):
                            eng.wait_ge(*act_aux.at(f"in{d}", n))
                            eng.wait_ge(stored[f"ar{d}"], n * 16)
                            nc.vector.tensor_tensor(arst[d][:, WAY[d], CH:], split(mr), split(e_in[:]), ALU.mult
                                                    ).then_inc(*dve_aux.inc(f"R{d}"))
                            eng.wait_ge(*act_aux.at(f"prev{d}", n))
                            nc.vector.tensor_tensor(arst[d][:, WAY[d], 0:CH], split(kk[:, s * SPAN:(s + 1) * SPAN]),
                                                    split(e_prev[:]), ALU.mult).then_inc(*dve_aux.inc(f"A{d}"))
                            eng.wait_ge(stored[f"kb{d}"], n * 16)
                            nc.vector.tensor_tensor(kbst[d][:, WAY[d], 0:CH], split(kd[d][:]), split(e_out[:]), ALU.mult
                                                    ).then_inc(*dve_aux.inc(f"K{d}"))
                            eng.wait_ge(*pool_aux.at(f"b{d}", n))
                            nc.vector.scalar_tensor_tensor(kbst[d][:, WAY[d], CH:], split(bv[d][:]), -1.0, split(e_out[:]),
                                                           ALU.mult, ALU.mult).then_inc(*dve_aux.inc(f"B{d}"))
                        eng.wait_ge(*pe_aux.at("BONUS", n))
                        eng.wait_ge(stored["b"], n * 16)
                        nc.vector.tensor_tensor(bst[:], pg[:], mv, ALU.mult).then_inc(*dve_aux.inc("bonus"))

                    for q in range(3):
                        mix(0, q, 0)
                    eng.wait_ge(act_low, 3)
                    for q in range(3):
                        mix(1, q, 1)
                    norm_max(0)
                    norm_kk(0, 1)
                    for j in range(PAIRS):
                        for s in range(SPANS):
                            aux(j, s, (j + 1) % 2, 3 * j + s == 0)
                            if j + 2 <= PAIRS:
                                mix(j + 2, s, j % 2)
                        if j + 1 < PAIRS:
                            eng.wait_ge(*pool_aux.at("b1", 3 * j + 2))
                            norm_max(j + 1)
                            norm_kk(j + 1, j % 2)

    def project_hgrn(self):
        nc = self.nc
        a = self.a
        HALF = (CH // 2 - 1, CH // 2)
        LAST = (CH - 1, 0)
        GUARD = 80.0
        TILE_OF = lambda h, q: (C_I, C_Q, C_F, C_F + DR, C_G)[q] + h * P
        with ExitStack() as ctx:
            sb = lambda n, s, dt=F32: ctx.enter_context(nc.sbuf_tensor(n, s, dt))
            psum = lambda n: ctx.enter_context(nc.psum_tensor(n, [P, SPAN], F32))
            wcol = [sb(f"h_wcol{q}", [P, KT, P]) for q in range(3)]
            iraw, qs, sg, fb, kf, lf, gi, rel = (sb("h_" + n, [P, T]) for n in
                                                 ("iraw", "qs", "sg", "f", "k", "lf", "gi", "rel"))
            eq, ek = sb("h_eq", [P, SPAN]), sb("h_ek", [P, SPAN])
            kqst = [sb(f"h_kqst{u}", [P, 2, CW, CH]) for u in range(2)]
            vst, gst = sb("h_vst", [P, SPAN]), sb("h_gst", [P, SPAN])
            restart = sb("h_restart", [P, SPAN])
            head, tail, dc = (sb("h_" + n, [P, CHUNKS]) for n in ("head", "tail", "dc"))
            lb0, lb1, lb, olb = (sb("h_" + n, [P, 2, PAIRS]) for n in ("lb0", "lb1", "lb", "olb"))
            pp = [psum(f"h_pp{s}") for s in range(6)]
            pv = psum("h_pv")

            params = self.sem("h_params")
            cleared = self.sem("h_cleared")
            setup = self.sem("h_setup")
            w_loaded = [self.sem(f"h_w_loaded{q}") for q in range(3)]
            kq_stored = [self.sem(f"h_kq_stored{u}") for u in range(2)]
            dc_stored, v_stored, g_stored = (self.sem(f"h_{n}_stored") for n in ("dc", "v", "g"))
            pe_proj = Marks(self.sem("h_pe_proj"), "p0 p1 p2")
            pe_v = Marks(self.sem("h_pe_v"), "v0 v1 v2")
            act_h = Marks(self.sem("h_act_h"), "i0 i1 i2 q0 q1 q2 v0 v1 v2 g0 g1 g2")
            act_f = Marks(self.sem("h_act_f"), "s0 s1 s2 ln0 ln1 ln2 eq0 ek0 eq1 ek1 eq2 ek2 dc")
            pool_f = Marks(self.sem("h_pool_f"), "k0 k1 k2")
            dve_f = Marks(self.sem("h_dve_f"), "f0 f1 f2 " + " ".join(
                f"scan{s} rel{s} head{s} tail{s} clamp{s}" for s in range(3)) + " join Q0 K0 Q1 K1 Q2 K2")
            split = lambda ap: ap.rearrange("p (c k) -> p c k", k=CH)
            span = lambda s: slice(s * SPAN, (s + 1) * SPAN)

            with nc.Block() as block:
                @block.sync
                def _(sp):
                    with nc.allow_non_contiguous_dma(reason="small weights, channel-major"):
                        for i, dst in ((0, lb0), (1, lb1)):
                            for d in range(2):
                                sp.dma_start(dst[:, d], a["hgrn_lb"][d, i].rearrange("(t p) -> p t", p=P)
                                             ).then_inc(params, 16)

                    def load_w(k):
                        if k >= 3:
                            self.hold_sp(sp, pe_proj.at("p2", k - 3))
                        c = TILE_OF(k // 5, k % 5)
                        sp.dma_start(wcol[k % 3][:], a["w_in"][0, :, c:c + P].rearrange("(k p) n -> p k n", p=P)
                                     ).then_inc(w_loaded[k % 3], 16)

                    for k in range(3):
                        load_w(k)
                    k = 3
                    for h in range(PAIRS):
                        for q in range(5):
                            if k < 5 * PAIRS:
                                load_w(k)
                                k += 1
                            if q == 1:
                                for s in range(SPANS):
                                    self.hold_sp(sp, act_h.at(f"v{s}", h))
                                    self.store_tokens(sp, self.itok, vst, s, slice(h * P, (h + 1) * P), v_stored)
                            if q in (2, 3):
                                d = q - 2
                                m = 2 * h + d
                                self.hold_sp(sp, act_f.at("dc", m))
                                sp.dma_start(self.hdecay[d, h], dc[:]).then_inc(dc_stored, 16)
                                for s in range(SPANS):
                                    self.hold_sp(sp, dve_f.at(f"K{s}", m))
                                    c0 = slot(d, s) * CW
                                    u = (3 * m + s) % 2
                                    sp.dma_start(self.kq[d, h, :, :, c0 * CH:(c0 + CW) * CH].rearrange("two p t -> p two t"),
                                                 kqst[u][:].rearrange("p two c k -> p two (c k)")
                                                 ).then_inc(kq_stored[u], 16)
                            if q == 4:
                                for s in range(SPANS):
                                    self.hold_sp(sp, act_h.at(f"g{s}", h))
                                    sp.dma_start(self.hgate[h, :, span(s)], gst[:]).then_inc(g_stored, 16)
                    for u in range(2):
                        sp.wait_ge(kq_stored[u], 16 * 3 * PAIRS)
                    sp.wait_ge(dc_stored, 16 * 2 * PAIRS)
                    sp.wait_ge(v_stored, 16 * 5 * 3 * PAIRS)
                    sp.wait_ge(g_stored, 16 * 3 * PAIRS)

                def read_of(k, s):
                    h, q = k // 5, k % 5
                    return (act_h.at(f"i{s}", h), act_h.at(f"q{s}", h), act_f.at(f"s{s}", 2 * h),
                            act_f.at(f"s{s}", 2 * h + 1), act_h.at(f"g{s}", h))[q]

                @block.tensor
                def _(eng):
                    for k in range(5 * PAIRS):
                        h, q = k // 5, k % 5
                        for s in range(SPANS):
                            if s == 0:
                                eng.wait_ge(w_loaded[k % 3], (k // 3 + 1) * 16)
                            if k >= 2:
                                eng.wait_ge(*read_of(k - 2, s))
                            for c in range(KT):
                                last = nc.tensor.matmul(pp[k % 2 * 3 + s][:], wcol[k % 3][:, c], self.hT[:, c, span(s)],
                                                        start=c == 0, stop=c == KT - 1)
                            last.then_inc(*pe_proj.inc(f"p{s}"))
                        if q == 1:
                            for s in range(SPANS):
                                eng.wait_ge(*act_h.at(f"i{s}", h))
                                if s:
                                    eng.wait_ge(*act_h.at(f"v{s - 1}", h))
                                elif h:
                                    eng.wait_ge(*act_h.at("v2", h - 1))
                                for i in range(SPAN // P):
                                    t = s * SPAN + i * P
                                    last = nc.tensor.transpose(pv[:, i * P:(i + 1) * P], iraw[:, t:t + P], self.ident[:])
                                last.then_inc(*pe_v.inc(f"v{s}"))

                @block.scalar
                def _(eng):
                    eng.wait_ge(setup, 1)
                    nc.scalar.activation(lb[:], lb0[:], ACT.Sigmoid).then_inc(setup, 1)
                    for k in range(5 * PAIRS):
                        h, q = k // 5, k % 5
                        for s in range(SPANS):
                            src = pp[k % 2 * 3 + s][:]
                            if q in (0, 1):
                                eng.wait_ge(*pe_proj.at(f"p{s}", k))
                                if h:
                                    eng.wait_ge(*(pe_v.at(f"v{s}", h - 1) if q == 0 else dve_f.at(f"Q{s}", 2 * h - 1)))
                                nc.scalar.activation((iraw, qs)[q][:, span(s)], src, (ACT.Copy, ACT.Silu)[q]
                                                     ).then_inc(*act_h.inc(f"{'iq'[q]}{s}"))
                            elif q == 4:
                                eng.wait_ge(*pe_proj.at(f"p{s}", k))
                                eng.wait_ge(g_stored, 16 * (3 * h + s))
                                nc.scalar.activation(gst[:], src, ACT.Silu).then_inc(*act_h.inc(f"g{s}"))
                        if q == 1:
                            for s in range(SPANS):
                                eng.wait_ge(*pe_v.at(f"v{s}", h))
                                eng.wait_ge(v_stored, 16 * 5 * (3 * h + s))
                                nc.scalar.activation(vst[:], pv[:], ACT.Copy).then_inc(*act_h.inc(f"v{s}"))
                        if q in (2, 3):
                            m = 2 * h + q - 2
                            for s in range(SPANS):
                                eng.wait_ge(*pe_proj.at(f"p{s}", k))
                                if m:
                                    eng.wait_ge(*dve_f.at(f"f{s}", m - 1))
                                nc.scalar.activation(sg[:, span(s)], pp[k % 2 * 3 + s][:], ACT.Sigmoid
                                                     ).then_inc(*act_f.inc(f"s{s}"))
                            for s in range(SPANS):
                                eng.wait_ge(*dve_f.at(f"f{s}", m))
                                if m:
                                    eng.wait_ge(*dve_f.at(f"scan{s}", m - 1))
                                nc.scalar.activation(lf[:, span(s)], fb[:, span(s)], ACT.Ln).then_inc(*act_f.inc(f"ln{s}"))
                            for s in range(SPANS):
                                eng.wait_ge(*dve_f.at(f"clamp{s}", m))
                                if s:
                                    eng.wait_ge(*dve_f.at(f"K{s - 1}", m))
                                elif m:
                                    eng.wait_ge(*dve_f.at("K2", m - 1))
                                nc.scalar.activation(eq[:], rel[:, span(s)], ACT.Exp).then_inc(*act_f.inc(f"eq{s}"))
                                nc.scalar.activation(ek[:], rel[:, span(s)], ACT.Exp, scale=-1.0
                                                     ).then_inc(*act_f.inc(f"ek{s}"))
                            eng.wait_ge(*dve_f.at("join", m))
                            eng.wait_ge(dc_stored, 16 * m)
                            nc.scalar.activation(dc[:], head[:], ACT.Exp).then_inc(*act_f.inc("dc"))

                @block.gpsimd
                def _(pool):
                    nc.gpsimd.memset(restart[:], 1.0).then_inc(cleared, 1)
                    pool.wait_ge(cleared, 1)
                    nc.gpsimd.memset(split(restart[:])[:, :, 0:1], 0.0).then_inc(cleared, 1)
                    for m in range(2 * PAIRS):
                        for s in range(SPANS):
                            pool.wait_ge(*dve_f.at(f"f{s}", m))
                            if m:
                                pool.wait_ge(*dve_f.at(f"K{s}", m - 1))
                            nc.gpsimd.tensor_scalar(kf[:, span(s)], fb[:, span(s)], -1.0, 1.0, ALU.mult, ALU.add
                                                    ).then_inc(*pool_f.inc(f"k{s}"))

                @block.vector
                def _(eng):
                    eng.wait_ge(params, 64)
                    nc.vector.tensor_tensor(lb0[:], lb0[:], lb1[:], ALU.subtract).then_inc(setup, 1)
                    eng.wait_ge(setup, 2)
                    nc.vector.tensor_scalar(olb[:], lb[:], -1.0, 1.0, ALU.mult, ALU.add).then_inc(setup, 1)
                    eng.wait_ge(setup, 3)
                    eng.wait_ge(cleared, 2)
                    for m in range(2 * PAIRS):
                        h, d = m // 2, m % 2
                        for s in range(SPANS):
                            eng.wait_ge(*act_f.at(f"s{s}", m))
                            if m:
                                eng.wait_ge(*act_f.at(f"ln{s}", m - 1))
                                eng.wait_ge(*pool_f.at(f"k{s}", m - 1))
                            nc.vector.tensor_scalar(fb[:, span(s)], sg[:, span(s)], olb[:, d, h:h + 1],
                                                    lb[:, d, h:h + 1], ALU.mult, ALU.add).then_inc(*dve_f.inc(f"f{s}"))
                        for s in range(SPANS):
                            eng.wait_ge(*act_f.at(f"ln{s}", m))
                            g = gi[:, span(s)]
                            nc.vector.tensor_tensor_scan(g[:, WAY[d]], restart[:], lf[:, span(s)][:, WAY[d]], 0.0,
                                                         ALU.mult, ALU.add).then_inc(*dve_f.inc(f"scan{s}"))
                            eng.wait_ge(*dve_f.at(f"scan{s}", m))
                            if m:
                                eng.wait_ge(*act_f.at(f"ek{s}", m - 1))
                            r = split(rel[:, span(s)])
                            middle = split(g)[:, :, HALF[d]:HALF[d] + 1]
                            nc.vector.tensor_tensor(r, split(g), middle.broadcast_to((P, CW, CH)), ALU.subtract
                                                    ).then_inc(*dve_f.inc(f"rel{s}"))
                            steps = slice(slot(d, s) * CW, (slot(d, s) + 1) * CW)
                            if s == 0 and m:
                                eng.wait_ge(*act_f.at("dc", m - 1))
                            nc.vector.tensor_copy(head[:, steps][:, WAY[d]].unsqueeze(2), middle
                                                  ).then_inc(*dve_f.inc(f"head{s}"))
                            eng.wait_ge(*dve_f.at(f"rel{s}", m))
                            nc.vector.tensor_copy(tail[:, steps][:, WAY[d]].unsqueeze(2), r[:, :, LAST[d]:LAST[d] + 1]
                                                  ).then_inc(*dve_f.inc(f"tail{s}"))
                            eng.wait_ge(*dve_f.at(f"tail{s}", m))
                            nc.vector.tensor_scalar(rel[:, span(s)], rel[:, span(s)], GUARD, -GUARD, ALU.min, ALU.max
                                                    ).then_inc(*dve_f.inc(f"clamp{s}"))
                        eng.wait_ge(*dve_f.at("clamp2", m))
                        nc.vector.tensor_tensor(head[:, 1:], head[:, 1:], tail[:, :-1], ALU.add
                                                ).then_inc(*dve_f.inc("join"))
                        for s in range(SPANS):
                            n = 3 * m + s
                            out = kqst[n % 2]
                            eng.wait_ge(*act_f.at(f"ek{s}", m))
                            eng.wait_ge(*pool_f.at(f"k{s}", m))
                            eng.wait_ge(*act_h.at(f"q{s}", h))
                            eng.wait_ge(kq_stored[n % 2], 16 * (n // 2))
                            nc.vector.tensor_tensor(out[:, 1, WAY[d]], split(qs[:, span(s)]), split(eq[:]), ALU.mult
                                                    ).then_inc(*dve_f.inc(f"Q{s}"))
                            nc.vector.tensor_tensor(out[:, 0, WAY[d]], split(kf[:, span(s)]), split(ek[:]), ALU.mult
                                                    ).then_inc(*dve_f.inc(f"K{s}"))

    def stepped(self, eng, front, back, bufs=2):
        front(0, 0)
        both = lambda c, u: back(c, u, c + 1, (u + 1) % bufs)
        peeled = (self.steps - 1) % bufs or bufs
        turns = (self.steps - 1 - peeled) // bufs
        for c in range(peeled):
            both(c, c % bufs)
        with eng.Fori(0, turns) as turn:
            for k in range(bufs):
                both(turn * bufs + (peeled + k), (peeled + k) % bufs)
        back(self.steps - 1, (self.steps - 1) % bufs, None, None)

    def mix_rwkv(self):
        nc = self.nc
        G = 2 * PAIRS
        self.steps = CHUNKS
        AHEAD = 4
        with ExitStack() as ctx:
            sb = lambda n, s, dt=F32: ctx.enter_context(nc.sbuf_tensor(n, s, dt))
            psum = lambda n, w: ctx.enter_context(nc.psum_tensor(n, [P, G, w], F32))
            kbd = [sb(f"m_kb{u}", [P, G, P]) for u in range(AHEAD)]
            arb = [sb(f"m_ar{u}", [P, G, 2 * CH]) for u in range(AHEAD)]
            vz = [sb(f"m_v{u}", [P, G, RH]) for u in range(AHEAD)]
            kbt = [sb(f"m_kbt{u}", [P, G, P]) for u in range(2)]
            sm = [sb(f"m_sm{u}", [P, G, 2 * CH]) for u in range(2)]
            xt = [sb(f"m_xt{u}", [P, G, CH]) for u in range(2)]
            z = [sb(f"m_z{u}", [P, G, RH]) for u in range(2)]
            state = [sb(f"m_state{u}", [P, G, RH]) for u in range(2)]
            pw = sb("m_pw", [P, G, CH])
            px = sb("m_px", [P, G, 2 * CH])
            rs = sb("m_rs", [P, G, RH])
            grown = sb("m_grown", [P, G, RH])
            mask = sb("m_mask", [P, 2, 2 * CH])
            eye = sb("m_eye", [P, CH])
            decay = sb("m_decay", [P, G, CHUNKS])
            oacc = sb("m_oacc", [P, G, T])
            ps_s, ps_i, ps_r, ps_u, ps_m = (psum("m_ps_" + n, RH) for n in "sirum")
            ps_o = psum("m_ps_o", CH)

            filled = self.sem("m_filled")
            cleared = self.sem("m_cleared")
            decay_loaded = self.sem("m_decay_loaded")
            loaded = [self.sem(f"m_loaded{u}") for u in range(AHEAD)]
            out_stored = self.sem("m_out_stored")
            pe_f = Marks(self.sem("m_pe_front"), "S I0 I1 I2 I3 I4")
            dve_f = Marks(self.sem("m_dve_front"), "mask P0 X0 P1 turn1 X1 P2 turn2 kbt X2 P3 turn3 X3 P4 turn4 X4")
            pe_b = Marks(self.sem("m_pe_back"), "R U M O")
            act_b = Marks(self.sem("m_act_back"), "R O")
            dve_b = Marks(self.sem("m_dve_back"), "Z grown state")

            with nc.Block() as block:
                @block.gpsimd
                def _(pool):
                    for u in range(AHEAD):
                        nc.gpsimd.memset(kbd[u][:], 0.0).then_inc(filled, 1)
                        nc.gpsimd.memset(vz[u][:], 0.0).then_inc(filled, 1)
                    for u in range(2):
                        nc.gpsimd.memset(kbt[u][:], 0.0).then_inc(filled, 1)
                    nc.gpsimd.memset(state[0][:], 0.0).then_inc(filled, 1)
                    nc.gpsimd.memset(mask[:], 1.0).then_inc(filled, 1)
                    nc.gpsimd.memset(eye[:], 0.0).then_inc(filled, 1)
                    pool.wait_ge(filled, 2 * AHEAD + 5)
                    for q in range(P // CH):
                        r = slice(q * CH, (q + 1) * CH)
                        nc.gpsimd.affine_select(out=eye[r], in_=eye[r], compare_op=ALU.not_equal, fill=1.0, base=0,
                                                pattern=[[-1, CH]], channel_multiplier=1).then_inc(filled, 1)
                        for d, sign in ((0, 1), (1, -1)):
                            for part, op in ((0, ALU.is_gt), (1, ALU.is_ge)):
                                m = mask[r, d, part * CH:(part + 1) * CH]
                                nc.gpsimd.affine_select(out=m, in_=m, compare_op=op, fill=0.0, base=0,
                                                        pattern=[[sign, CH]], channel_multiplier=-sign
                                                        ).then_inc(filled, 1)

                FILLED = 2 * AHEAD + 5 + 5 * (P // CH)

                @block.sync
                def _(sp):
                    sp.wait_ge(filled, FILLED)
                    sp.dma_start(decay[:], self.rdecay.rearrange("d j p c -> p (d j) c")).then_inc(decay_loaded, 16)

                    def load(c, u):
                        self.hold_sp(sp, pe_b.ago("O", c, AHEAD), dve_f.ago("kbt", c, AHEAD))
                        kbv = self.kb.rearrange("d j p c n -> p (d j) c n")
                        arv = self.ar.rearrange("d j p c n -> p (d j) c n")
                        vv = self.vtok.rearrange("d (c s) (j h v) -> c h s d j v", s=CH, j=PAIRS, h=2)
                        for h in range(2):
                            r = slice(RH * h, RH * h + RH)
                            sp.dma_start(kbd[u][r, :, r], kbv[r, :, bass.ds(c, 1)].rearrange("p g o n -> p g (o n)")
                                         ).then_inc(loaded[u], 16)
                            for d in range(2):
                                sp.dma_start(vz[u][RH * h:RH * h + CH, d * PAIRS:(d + 1) * PAIRS],
                                             vv[bass.ds(c, 1), h, :, d].rearrange("o s j v -> (o s) j v")
                                             ).then_inc(loaded[u], 16)
                        sp.dma_start(arb[u][:], arv[:, :, bass.ds(c, 1)].rearrange("p g o n -> p g (o n)")
                                     ).then_inc(loaded[u], 16)
                    for c in range(AHEAD):
                        load(c, c)

                    def store(c0, c1):
                        self.hold_sp(sp, act_b.at("O", c1 - 1))
                        t = slice(c0 * CH, c1 * CH)
                        for g in range(G):
                            sp.dma_start(self.yT[g // PAIRS, g % PAIRS, :, t], oacc[:, g, t]).then_inc(out_stored, 16)
                    first = SEQ_P // CH
                    for lo, hi in ((1, first // AHEAD + 1), (first // AHEAD + 1, CHUNKS // AHEAD)):
                        with sp.Fori(lo, hi) as turn:
                            for u in range(AHEAD):
                                load(turn * AHEAD + u, u)
                        if lo == 1:
                            store(0, first)
                    store(first, CHUNKS)
                    sp.wait_ge(out_stored, 2 * 16 * G)

                LOADS = 16 * 7

                @block.tensor
                def _(eng):
                    eng.wait_ge(filled, FILLED)
                    eng.wait_ge(cleared, 3)

                    heads, k_quarters, b_quarters = ([slice(RH * h + a, RH * h + b) for h in range(2)]
                                                     for a, b in ((0, RH), (0, CH), (CH, RH)))

                    def quarters():
                        return [(g, slice(q * CH, (q + 1) * CH), slice(q // 2 * RH, q // 2 * RH + RH))
                                for g in range(G) for q in (0, 2, 1, 3)]

                    def scores(c, u):
                        self.hold_pe(eng, (loaded[u], (c - u) * (LOADS // AHEAD) + LOADS), dve_f.ago("mask", c, 1))
                        for g, q, r in quarters():
                            last = nc.tensor.matmul(ps_s[q, g], kbd[u][r, g, q], arb[u][r, g], start=True, stop=True)
                        last.then_inc(*pe_f.inc("S"))

                    def units():
                        return [(slice(CH + RH * h, 2 * CH + RH * h), g) for g in range(G) for h in range(2)]

                    def power(c, u, i):
                        if i == 0:
                            self.hold_pe(eng, dve_f.at("P0", c), dve_f.ago("X4", c, 1))
                        else:
                            self.hold_pe(eng, dve_f.at(f"turn{i}", c))
                        for q, g in units():
                            if i == 0:
                                last = nc.tensor.matmul(ps_i[q, g, 0:CH], pw[q, g], sm[u % 2][q, g, 0:CH], start=True,
                                                        stop=True)
                            elif i < 4:
                                last = nc.tensor.matmul(ps_i[q, g], pw[q, g], px[q, g], start=True, stop=True)
                            else:
                                last = nc.tensor.matmul(ps_i[q, g, CH:], pw[q, g], px[q, g, CH:], start=True, stop=True)
                        last.then_inc(*pe_f.inc(f"I{i}"))

                    def back(c, u, f, v):
                        if f is not None:
                            scores(f, v)
                        self.hold_pe(eng, dve_b.ago("state", c, 1), act_b.ago("R", c, 1), dve_f.at("mask", c))
                        for g in range(G):
                            for r, k, q in zip(heads, k_quarters, b_quarters):
                                nc.tensor.matmul(ps_r[q, g], arb[u][r, g, 0:CH], state[u % 2][r, g], start=True,
                                                 stop=False)
                            for r, k, q in zip(heads, k_quarters, b_quarters):
                                last = nc.tensor.matmul(ps_r[q, g], sm[u % 2][k, g, 0:CH], vz[u][k, g], start=False,
                                                        stop=True)
                        last.then_inc(*pe_b.inc("R"))
                        if f is not None:
                            power(f, v, 0)
                        self.hold_pe(eng, act_b.at("R", c), dve_f.at("X4", c), dve_b.ago("Z", c, 1))
                        for q, g in units():
                            last = nc.tensor.matmul(ps_u[q, g], xt[u % 2][q, g], rs[q, g], start=True, stop=True)
                        last.then_inc(*pe_b.inc("U"))
                        if f is not None:
                            power(f, v, 1)
                        self.hold_pe(eng, dve_b.at("Z", c), dve_f.at("kbt", c), dve_b.ago("grown", c, 1))
                        for g, q, r in quarters():
                            last = nc.tensor.matmul(ps_m[q, g], kbt[u % 2][r, g, q], z[u % 2][r, g], start=True,
                                                    stop=True)
                        last.then_inc(*pe_b.inc("M"))
                        if f is not None:
                            power(f, v, 2)
                        self.hold_pe(eng, act_b.ago("O", c, 1))
                        for g in range(G):
                            for r in heads:
                                nc.tensor.matmul(ps_o[r, g], state[u % 2][r, g], arb[u][r, g, CH:], start=True,
                                                 stop=False)
                            for r in heads:
                                last = nc.tensor.matmul(ps_o[r, g], z[u % 2][r, g], sm[u % 2][r, g, CH:], start=False,
                                                        stop=True)
                        last.then_inc(*pe_b.inc("O"))
                        if f is not None:
                            power(f, v, 3)
                            power(f, v, 4)

                    def front(c, u):
                        scores(c, u)
                        for i in range(5):
                            power(c, u, i)
                    self.stepped(eng, front, back, AHEAD)

                @block.scalar
                def _(eng):
                    def back(c, u, f, v):
                        self.waits(eng, pe_b.at("R", c))
                        nc.scalar.activation(rs[:], ps_r[:], ACT.Copy).then_inc(*act_b.inc("R"))
                        self.waits(eng, pe_b.at("O", c))
                        nc.scalar.activation(oacc[:, :, bass.ds(c * CH, CH)], ps_o[:], ACT.Copy
                                             ).then_inc(*act_b.inc("O"))
                    self.waits(eng, (cleared, 3))
                    self.stepped(eng, lambda c, u: None, back, AHEAD)

                @block.vector
                def _(eng):
                    for ps in (ps_i, ps_r, ps_u):
                        nc.vector.memset(ps[:], 0.0).then_inc(cleared, 1)
                    eng.wait_ge(filled, FILLED)
                    eng.wait_ge(decay_loaded, 16)
                    nc.vector.memset(decay[:, :, SEQ_P // CH - 1:SEQ_P // CH], 0.0).then_inc(cleared, 1)
                    eng.wait_ge(cleared, 4)

                    def masks(c, u):
                        self.waits(eng, pe_f.at("S", c), pe_b.ago("O", c, 2))
                        by_way = lambda ap: ap.rearrange("p (d j) n -> p d j n", d=2)
                        nc.vector.tensor_tensor(by_way(sm[u % 2][:]), by_way(ps_s[:]),
                                                mask[:].unsqueeze(2).broadcast_to((P, 2, PAIRS, 2 * CH)), ALU.mult
                                                ).then_inc(*dve_f.inc("mask"))
                        self.waits(eng, dve_f.at("mask", c), pe_f.ago("I4", c, 1), dve_f.ago("X4", c, 1))
                        nc.vector.transpose(pw[:], sm[u % 2][:, :, 0:CH]).then_inc(*dve_f.inc("P0"))
                        nc.vector.tensor_tensor(px[:, :, CH:], sm[u % 2][:, :, 0:CH],
                                                eye[:].unsqueeze(1).broadcast_to((P, G, CH)), ALU.add
                                                ).then_inc(*dve_f.inc("X0"))

                    def power(c, u, i):
                        self.waits(eng, pe_f.at(f"I{i - 1}", c))
                        if i > 1:
                            nc.vector.tensor_tensor(px[:, :, CH:], px[:, :, CH:], ps_i[:, :, CH:], ALU.add
                                                    ).then_inc(*dve_f.inc(f"X{i - 1}"))
                        nc.vector.tensor_copy(px[:, :, 0:CH], ps_i[:, :, 0:CH]).then_inc(*dve_f.inc(f"P{i}"))
                        self.waits(eng, dve_f.at(f"P{i}", c))
                        nc.vector.transpose(pw[:], px[:, :, 0:CH]).then_inc(*dve_f.inc(f"turn{i}"))

                    def turn_kb(c, u):
                        self.waits(eng, (loaded[u], (c - u) * (LOADS // AHEAD) + LOADS), pe_b.ago("M", c, 2))
                        for h in range(2):
                            for i in range(RH * h, RH * h + RH, CH):
                                for j in range(RH * h, RH * h + RH, CH):
                                    last = nc.vector.transpose(kbt[u % 2][j:j + CH, :, i:i + CH],
                                                               kbd[u][i:i + CH, :, j:j + CH])
                        last.then_inc(*dve_f.inc("kbt"))

                    def inverse(c, u):
                        self.waits(eng, pe_f.at("I4", c), pe_b.ago("U", c, 2))
                        nc.vector.tensor_tensor(xt[u % 2][:], px[:, :, CH:], ps_i[:, :, CH:], ALU.add
                                                ).then_inc(*dve_f.inc("X4"))

                    def front(c, u):
                        masks(c, u)
                        for i in range(1, 5):
                            power(c, u, i)
                            if i == 2:
                                turn_kb(c, u)
                        inverse(c, u)

                    def back(c, u, f, v):
                        if f is not None:
                            masks(f, v)
                            power(f, v, 1)
                        self.waits(eng, pe_b.at("U", c))
                        nc.vector.tensor_tensor(z[u % 2][:], ps_u[:], vz[u][:], ALU.add).then_inc(*dve_b.inc("Z"))
                        if f is not None:
                            power(f, v, 2)
                            turn_kb(f, v)
                        self.waits(eng, pe_b.at("M", c))
                        nc.vector.tensor_tensor(grown[:], ps_m[:], state[u % 2][:], ALU.add).then_inc(*dve_b.inc("grown"))
                        self.waits(eng, dve_b.at("grown", c))
                        nc.vector.tensor_tensor(state[1 - u % 2][:], grown[:],
                                                decay[:, :, bass.ds(c, 1)].broadcast_to((P, G, RH)), ALU.mult
                                                ).then_inc(*dve_b.inc("state"))
                        if f is not None:
                            power(f, v, 3)
                            power(f, v, 4)
                            inverse(f, v)
                    self.stepped(eng, front, back, AHEAD)

    def mix_hgrn(self):
        nc = self.nc
        G = 2 * PAIRS
        NC = P // CH
        self.steps = TILES
        with ExitStack() as ctx:
            sb = lambda n, s, dt=F32: ctx.enter_context(nc.sbuf_tensor(n, s, dt))
            psum = lambda n, w: ctx.enter_context(nc.psum_tensor(n, [P, G, w], F32))
            kq = [sb(f"g_kq{u}", [P, 2, G, P]) for u in range(2)]
            v = [sb(f"g_v{u}", [P, 2, DR]) for u in range(2)]
            pt = [sb(f"g_pt{u}", [P, G, P]) for u in range(2)]
            kt = [sb(f"g_kt{u}", [P, G, P]) for u in range(2)]
            s = [sb(f"g_s{n}", [P, G, P]) for n in range(2)]
            y = sb("g_y", [P, G, P])
            mask = sb("g_mask", [P, 2, P])
            decay = sb("g_decay", [P, G, CHUNKS])
            oacc = sb("g_oacc", [P, G, T])
            ps_s, ps_t, ps_kv, ps_o = (psum("g_ps_" + n, P) for n in ("s", "t", "kv", "o"))

            filled = self.sem("g_filled")
            cleared = self.sem("g_cleared")
            decay_loaded = self.sem("g_decay_loaded")
            loaded = [self.sem(f"g_loaded{u}") for u in range(2)]
            out_stored = self.sem("g_out_stored")
            pe_f = Marks(self.sem("g_pe_front"), "S T")
            act_f = Marks(self.sem("g_act_front"), "kt")
            dve_f = Marks(self.sem("g_dve_front"), "mask")
            pe_b = Marks(self.sem("g_pe_back"), "kv0 o0 kv1 o1 kv2 o2 kv3 o3")
            act_b = Marks(self.sem("g_act_back"), "O")
            dve_b = Marks(self.sem("g_dve_back"), "s0 y0 s1 y1 s2 y2 s3 y3")
            FILLED = 1 + 2 * NC

            with nc.Block() as block:
                @block.gpsimd
                def _(pool):
                    nc.gpsimd.memset(mask[:], 1.0).then_inc(filled, 1)
                    pool.wait_ge(filled, 1)
                    for q in range(NC):
                        r = slice(q * CH, (q + 1) * CH)
                        for d, sign in ((0, 1), (1, -1)):
                            m = mask[r, d, r]
                            nc.gpsimd.affine_select(out=m, in_=m, compare_op=ALU.is_ge, fill=0.0,
                                                    base=0, pattern=[[sign, CH]], channel_multiplier=-sign
                                                    ).then_inc(filled, 1)

                @block.sync
                def _(sp):
                    sp.dma_start(decay[:], self.hdecay.rearrange("d j p c -> p (d j) c")).then_inc(decay_loaded, 16)

                    def load(c, u):
                        self.hold_sp(sp, pe_b.ago("o3", c, 2), pe_f.ago("T", c, 2))
                        kqv = self.kq.rearrange("d j two p t -> p two (d j) t")
                        for i in range(2):
                            sp.dma_start(kq[u][:, i], kqv[:, i, :, bass.ds(c * P, P)]).then_inc(loaded[u], 16)
                        sp.dma_start(v[u][:], self.itok[:, bass.ds(c * P, P)].rearrange("d t n -> t d n")
                                     ).then_inc(loaded[u], 16)
                    load(0, 0)
                    load(1, 1)

                    def store(c0, c1):
                        self.hold_sp(sp, act_b.at("O", c1 - 1))
                        t = slice(c0 * P, c1 * P)
                        for g in range(G):
                            sp.dma_start(self.yT[g // PAIRS, PAIRS + g % PAIRS, :, t], oacc[:, g, t]
                                         ).then_inc(out_stored, 16)
                    first = SEQ_P // P
                    for lo, hi in ((0, first // 2), (first // 2, TILES // 2 - 1)):
                        with sp.Fori(lo, hi) as half:
                            load(half * 2 + 2, 0)
                            load(half * 2 + 3, 1)
                        if lo == 0:
                            store(0, first)
                    store(first, TILES)
                    sp.wait_ge(out_stored, 2 * 16 * G)

                @block.tensor
                def _(eng):
                    eng.wait_ge(cleared, 2)
                    def scores(c, u):
                        self.hold_pe(eng, (loaded[u], (c - u) * 24 + 48), dve_f.ago("mask", c, 1))
                        for g in range(G):
                            for n in range(NC):
                                r = slice(n * CH, (n + 1) * CH)
                                last = nc.tensor.matmul(ps_s[r, g, r], kq[u][:, 0, g, r], kq[u][:, 1, g, r], start=True,
                                                        stop=True)
                        last.then_inc(*pe_f.inc("S"))

                    def turn_k(c, u):
                        self.hold_pe(eng, act_f.ago("kt", c, 1))
                        for g in range(G):
                            last = nc.tensor.transpose(ps_t[:, g], kq[u][:, 0, g], self.ident[:])
                        last.then_inc(*pe_f.inc("T"))

                    def front(c, u):
                        scores(c, u)
                        turn_k(c, u)

                    def back(c, u, f, w):
                        for n in range(NC):
                            r = slice(n * CH, (n + 1) * CH)
                            self.hold_pe(eng, dve_b.ago("y3", c, 1) if n == 0 else dve_b.at(f"y{n - 1}", c),
                                         *((act_f.at("kt", c), dve_f.at("mask", c), act_b.ago("O", c, 1))
                                           if n == 0 else ()))
                            for g in range(G):
                                vg = v[u][r, g // PAIRS, g % PAIRS * P:(g % PAIRS + 1) * P]
                                last = nc.tensor.matmul(ps_kv[:, g], kt[u][r, g], vg, start=True, stop=True)
                            last.then_inc(*pe_b.inc(f"kv{n}"))
                            if f is not None and n == 1:
                                scores(f, w)
                            if f is not None and n == 2:
                                turn_k(f, w)
                            if n == 0:
                                for g in range(G):
                                    vg = v[u][:, g // PAIRS, g % PAIRS * P:(g % PAIRS + 1) * P]
                                    nc.tensor.matmul(ps_o[:, g], vg, pt[u][:, g], start=g % 4 == 0, stop=False,
                                                     skip_group_check=True)
                            self.hold_pe(eng, dve_b.at(f"s{n}", c))
                            for g in range(G):
                                last = nc.tensor.matmul(ps_o[:, g, r], s[n % 2][:, g], kq[u][:, 1, g, r], start=False,
                                                        stop=n == NC - 1, skip_group_check=True)
                            last.then_inc(*pe_b.inc(f"o{n}"))
                    self.stepped(eng, front, back)

                @block.scalar
                def _(eng):
                    def turn_k(c, u):
                        self.waits(eng, pe_f.at("T", c), pe_b.ago("kv3", c, 2))
                        nc.scalar.activation(kt[u][:], ps_t[:], ACT.Copy).then_inc(*act_f.inc("kt"))

                    def back(c, u, f, w):
                        if f is not None:
                            turn_k(f, w)
                        self.waits(eng, pe_b.at("o3", c))
                        nc.scalar.activation(oacc[:, :, bass.ds(c * P, P)], ps_o[:], ACT.Copy
                                             ).then_inc(*act_b.inc("O"))
                    self.stepped(eng, turn_k, back)

                @block.vector
                def _(eng):
                    nc.vector.memset(y[:], 0.0).then_inc(cleared, 1)
                    nc.vector.memset(ps_s[:], 0.0).then_inc(cleared, 1)
                    eng.wait_ge(filled, FILLED)
                    eng.wait_ge(decay_loaded, 16)
                    nc.vector.memset(decay[:, :, SEQ_P // CH:SEQ_P // CH + 1], 0.0).then_inc(cleared, 1)
                    eng.wait_ge(cleared, 3)

                    def masks(c, u):
                        self.waits(eng, pe_f.at("S", c), pe_b.ago("o3", c, 2))
                        by_way = lambda ap: ap.rearrange("p (d j) n -> p d j n", d=2)
                        nc.vector.tensor_tensor(by_way(pt[u][:]), by_way(ps_s[:]),
                                                mask[:].unsqueeze(2).broadcast_to((P, 2, PAIRS, P)), ALU.mult
                                                ).then_inc(*dve_f.inc("mask"))

                    def back(c, u, f, w):
                        for n in range(NC):
                            self.waits(eng, dve_b.ago("y3", c, 1) if n == 0 else dve_b.at(f"y{n - 1}", c),
                                       pe_b.at(f"o{n - 2}", c) if n > 1 else pe_b.ago(f"o{n + 2}", c, 1))
                            nc.vector.tensor_tensor(s[n % 2][:], y[:],
                                                    decay[:, :, bass.ds(c * NC + n, 1)].broadcast_to((P, G, P)),
                                                    ALU.mult).then_inc(*dve_b.inc(f"s{n}"))
                            self.waits(eng, pe_b.at(f"kv{n}", c), dve_b.at(f"s{n}", c))
                            nc.vector.tensor_tensor(y[:], ps_kv[:], s[n % 2][:], ALU.add).then_inc(*dve_b.inc(f"y{n}"))
                            if f is not None and n == 1:
                                masks(f, w)
                    self.stepped(eng, masks, back)

    def mixer_out(self):
        nc = self.nc
        a = self.a
        EPS_R, EPS_H, EPS_2 = RH * 1e-5, 1e-5, 1e-6
        KY = 2 * PAIRS
        ITEMS = KY * SPANS
        with ExitStack() as ctx:
            sb = lambda n, s, dt=F32: ctx.enter_context(nc.sbuf_tensor(n, s, dt))
            y = sb("o_y", [P, KY, T])
            of, ob, bv, gt, sq, rt = ([sb(f"o_{n}{u}", [P, SPAN]) for u in range(2)]
                                      for n in ("of", "ob", "bv", "gt", "sq", "rt"))
            wout = sb("o_wout", [P, KY, D])
            wr = sb("o_wr", [P, KT, NG + NE])
            lnw, lnb, gn = sb("o_lnw", [P, PAIRS]), sb("o_lnb", [P, PAIRS]), sb("o_gn", [P, 1])
            n2w = sb("o_n2w", [P, D])
            rbias = sb("o_rbias", [P, NG + NE])
            x, x1, h2, h2T, junk = ([sb(f"o_{n}{u}", [P, D]) for u in range(2)] for n in ("x", "x1", "h2", "h2T", "j"))
            ss, rq, rr = (sb("o_" + n, [P, 2]) for n in ("ss", "rq", "rr"))
            ps_mean = ctx.enter_context(nc.psum_tensor("o_ps_mean", [P, SPAN], F32))
            ps_ss = ctx.enter_context(nc.psum_tensor("o_ps_ss", [P, SPAN], F32))
            ps_out = ctx.enter_context(nc.psum_tensor("o_ps_out", [P, D], F32))
            ps_t = ctx.enter_context(nc.psum_tensor("o_ps_t", [P, D], F32))
            ps_r = ctx.enter_context(nc.psum_tensor("o_ps_r", [P, NG + NE], F32))

            params = self.sem("o_params")
            wout_loaded = self.sem("o_wout_loaded")
            loaded = [self.sem(f"o_loaded{u}") for u in range(2)]
            x_loaded = [self.sem(f"o_x_loaded{u}") for u in range(2)]
            x1_stored = [self.sem(f"o_x1_stored{u}") for u in range(2)]
            h2_stored = [self.sem(f"o_h2_stored{u}") for u in range(2)]
            pe_r = Marks(self.sem("o_pe_r"), "mean")
            pe_n = Marks(self.sem("o_pe_n"), "ss")
            act_n = Marks(self.sem("o_act_n"), "sq root")
            dve_a = Marks(self.sem("o_dve_a"), "sum centre")
            dve_n = Marks(self.sem("o_dve_n"), "var inv norm scaled bonus gated")
            pe_t = Marks(self.sem("o_pe_t"), "out")
            pe_h = Marks(self.sem("o_pe_h"), "turned routed")
            act_t = Marks(self.sem("o_act_t"), "sq root")
            act_h = Marks(self.sem("o_act_h"), "turned")
            dve_t = Marks(self.sem("o_dve_t"), "x1 meansq inv h2")
            dve_h = Marks(self.sem("o_dve_h"), "logits")
            is_r = lambda n: n % KY < PAIRS
            rank = lambda n: n // KY * PAIRS + n % KY
            loads = [4 if is_r(n) else 3 for n in range(ITEMS)]
            loads_by = [sum(loads[n % 2:n + 1:2]) * 16 for n in range(ITEMS)]
            src = lambda t: a["x_prompt"][0, t * P:(t + 1) * P] if t * P < SEQ_P else \
                a["x_sample"][0, t * P - SEQ_P:(t + 1) * P - SEQ_P]

            def schedule(item, tile):
                for s in range(SPANS + 1):
                    for i in range(KY):
                        if s < SPANS:
                            item(KY * s + i)
                        if s and i % 2:
                            tile((s - 1) * (SPAN // P) + i // 2)
                tile(TILES)

            with nc.Block() as block:
                @block.sync
                def _(sp):
                    with nc.allow_non_contiguous_dma(reason="small weights"):
                        for dst, w in ((lnw[:], a["rwkv_lnx_w"][0].rearrange("(t p) -> p t", p=P)),
                                       (lnb[:], a["rwkv_lnx_b"][0].rearrange("(t p) -> p t", p=P)),
                                       (gn[:], a["hgrn_gnorm_w"][0].rearrange("(p o) -> p o", o=1)),
                                       (n2w[:], a["norm2_w"].partition_broadcast(P)),
                                       (rbias[:, 0:NG], a["router_group_b"].partition_broadcast(P)),
                                       (rbias[:, NG:], a["router_expert_b"].partition_broadcast(P)),
                                       (wr[:, :, 0:NG], a["router_group_w"][0].rearrange("(c p) n -> p c n", p=P)),
                                       (wr[:, :, NG:], a["router_expert_w"][0].rearrange("(c p) n -> p c n", p=P))):
                            sp.dma_start(dst, w).then_inc(params, 16)

                    def load(n):
                        u, s, i = n % 2, n // KY, n % KY
                        if n >= 2:
                            self.hold_sp(sp, dve_n.at("gated", n - 2))
                        t = slice(s * SPAN, (s + 1) * SPAN)
                        b = slice(slot(1, s) * SPAN, (slot(1, s) + 1) * SPAN)
                        sp.dma_start(of[u][:], self.yT[0, i, :, t]).then_inc(loaded[u], 16)
                        sp.dma_start(ob[u][:], self.yT[1, i, :, b]).then_inc(loaded[u], 16)
                        if is_r(n):
                            sp.dma_start(bv[u][:], self.bonusv[i, :, t]).then_inc(loaded[u], 16)
                            sp.dma_start(gt[u][:], self.rgate[i, :, t]).then_inc(loaded[u], 16)
                        else:
                            sp.dma_start(gt[u][:], self.hgate[i - PAIRS, :, t]).then_inc(loaded[u], 16)
                        if n == 1:
                            sp.dma_start(wout[:], a["w_out"][0].rearrange("(k p) n -> p k n", p=P)
                                         ).then_inc(wout_loaded, 16)

                    def tile(t):
                        u = t % 2
                        if t == TILES:
                            return
                        if t == 0:
                            load_x(0)
                        if t + 1 < TILES:
                            load_x(t + 1)
                        self.hold_sp(sp, dve_t.at("x1", t))
                        sp.dma_start(self.x1[t * P:(t + 1) * P], x1[u][:]).then_inc(x1_stored[u], 16)
                        self.hold_sp(sp, dve_t.at("h2", t))
                        sp.dma_start(self.h2[t * P:(t + 1) * P], h2[u][:]).then_inc(h2_stored[u], 16)

                    def load_x(t):
                        if t >= 2:
                            self.hold_sp(sp, dve_t.at("x1", t - 2))
                        sp.dma_start(x[t % 2][:], src(t)).then_inc(x_loaded[t % 2], 16)
                    load(0)
                    load(1)
                    schedule(lambda n: load(n + 2) if n + 2 < ITEMS else None, tile)
                    for u in range(2):
                        sp.wait_ge(x1_stored[u], TILES // 2 * 16)
                        sp.wait_ge(h2_stored[u], TILES // 2 * 16)

                @block.tensor
                def _(eng):
                    def mean(n):
                        u = n % 2
                        if is_r(n):
                            self.waits(eng, dve_a.at("sum", n), dve_a.at("centre", n - 1) if n else None)
                            nc.tensor.matmul(ps_mean[:], self.headsum[:], of[u][:], start=True, stop=True
                                             ).then_inc(*pe_r.inc("mean"))

                    def item(n):
                        u = n % 2
                        self.waits(eng, act_n.at("sq", n), dve_n.ago("var", n, 1))
                        nc.tensor.matmul(ps_ss[:], (self.headsum if is_r(n) else self.allsum)[:], sq[u][:],
                                         start=True, stop=True).then_inc(*pe_n.inc("ss"))
                        if n + 1 < ITEMS:
                            mean(n + 1)

                    def out(t):
                        if t == 0:
                            eng.wait_ge(wout_loaded, 16)
                        s = t * P // SPAN
                        self.waits(eng, dve_n.at("gated", KY * (s + 1) - 1), dve_t.ago("x1", t, 1))
                        for half in range(2):
                            for k in range(KY):
                                last = nc.tensor.matmul(ps_out[:, half * SPAN:(half + 1) * SPAN],
                                                        y[:, k, t * P:(t + 1) * P],
                                                        wout[:, k, half * SPAN:(half + 1) * SPAN],
                                                        start=k == 0, stop=k == KY - 1)
                        last.then_inc(*pe_t.inc("out"))

                    def route(t):
                        u = t % 2
                        self.waits(eng, dve_t.at("h2", t), act_h.ago("turned", t, 1))
                        for c in range(KT):
                            last = nc.tensor.transpose(ps_t[:, c * P:(c + 1) * P], h2[u][:, c * P:(c + 1) * P],
                                                       self.ident[:])
                        last.then_inc(*pe_h.inc("turned"))
                        self.waits(eng, act_h.at("turned", t), dve_h.ago("logits", t, 1), (params, 16 * 8))
                        for c in range(KT):
                            last = nc.tensor.matmul(ps_r[:], h2T[u][:, c * P:(c + 1) * P], wr[:, c], start=c == 0,
                                                    stop=c == KT - 1)
                        last.then_inc(*pe_h.inc("routed"))

                    def tile(t):
                        if t < TILES:
                            out(t)
                        if t:
                            route(t - 1)
                    mean(0)
                    schedule(item, tile)

                @block.scalar
                def _(eng):
                    def item(n):
                        u = n % 2
                        self.waits(eng, dve_a.at("centre", n), pe_n.ago("ss", n, 2))
                        nc.scalar.activation(sq[u][:], of[u][:], ACT.Square).then_inc(*act_n.inc("sq"))
                        self.waits(eng, dve_n.at("var", n))
                        nc.scalar.activation(rt[u][:], rt[u][:], ACT.Sqrt).then_inc(*act_n.inc("root"))

                    def tile(t):
                        if t:
                            turn(t - 1)
                        if t == TILES:
                            return
                        u = t % 2
                        self.waits(eng, dve_t.at("x1", t), dve_t.ago("meansq", t, 2))
                        nc.scalar.activation(junk[u][:], x1[u][:], ACT.Square, accum_out=ss[:, u:u + 1]
                                             ).then_inc(*act_t.inc("sq"))
                        self.waits(eng, dve_t.at("meansq", t))
                        nc.scalar.activation(rq[:, u:u + 1], rq[:, u:u + 1], ACT.Sqrt).then_inc(*act_t.inc("root"))

                    def turn(t):
                        self.waits(eng, pe_h.at("turned", t), pe_h.ago("routed", t, 2))
                        nc.scalar.activation(h2T[t % 2][:], ps_t[:], ACT.Copy).then_inc(*act_h.inc("turned"))
                    schedule(item, tile)

                @block.vector
                def _(eng):
                    eng.wait_ge(params, 16 * 8)
                    split = lambda ap: ap.rearrange("p (c k) -> p c k", k=CH)

                    def add(n):
                        u = n % 2
                        eng.wait_ge(loaded[u], loads_by[n])
                        nc.vector.tensor_tensor(split(of[u][:]), split(of[u][:]), split(ob[u][:])[:, ::-1], ALU.add
                                                ).then_inc(*dve_a.inc("sum"))

                    def centre(n):
                        u = n % 2
                        if is_r(n):
                            self.waits(eng, pe_r.at("mean", rank(n)))
                            nc.vector.scalar_tensor_tensor(of[u][:], ps_mean[:], -1.0 / RH, of[u][:], ALU.mult, ALU.add
                                                           ).then_inc(*dve_a.inc("centre"))
                        else:
                            self.waits(eng, dve_a.at("sum", n))
                            nc.vector.tensor_copy(rr[:, 1:2], gn[:]).then_inc(*dve_a.inc("centre"))

                    def item(n):
                        u, s, i = n % 2, n // KY, n % KY
                        self.waits(eng, pe_n.at("ss", n), dve_n.ago("norm", n, 2))
                        nc.vector.tensor_scalar(rt[u][:], ps_ss[:], 1.0 / (RH if is_r(n) else P),
                                                EPS_R if is_r(n) else EPS_H, ALU.mult, ALU.add
                                                ).then_inc(*dve_n.inc("var"))
                        if n + 1 < ITEMS:
                            add(n + 1)
                        self.waits(eng, act_n.at("root", n))
                        nc.vector.reciprocal(rt[u][:], rt[u][:]).then_inc(*dve_n.inc("inv"))
                        if n + 1 < ITEMS:
                            centre(n + 1)
                        self.waits(eng, dve_n.at("inv", n))
                        w = lnw[:, i:i + 1] if is_r(n) else gn[:]
                        nc.vector.scalar_tensor_tensor(of[u][:], of[u][:], w, rt[u][:], ALU.mult, ALU.mult
                                                       ).then_inc(*dve_n.inc("norm"))
                        self.waits(eng, dve_n.at("norm", n))
                        if is_r(n):
                            nc.vector.tensor_scalar(of[u][:], of[u][:], lnb[:, i:i + 1], None, ALU.add
                                                    ).then_inc(*dve_n.inc("scaled"))
                            self.waits(eng, dve_n.at("scaled", n))
                            nc.vector.tensor_tensor(of[u][:], of[u][:], bv[u][:], ALU.add
                                                    ).then_inc(*dve_n.inc("bonus"))
                            self.waits(eng, dve_n.at("bonus", n))
                            nc.vector.tensor_tensor(y[:, i, s * SPAN:(s + 1) * SPAN], of[u][:], gt[u][:], ALU.mult
                                                    ).then_inc(*dve_n.inc("gated"))
                        else:
                            nc.vector.tensor_tensor(y[:, i, s * SPAN:(s + 1) * SPAN], of[u][:], gt[u][:], ALU.mult
                                                    ).then_inc(dve_n.sem, 3)
                            for name in ("scaled", "bonus", "gated"):
                                dve_n.inc(name)

                    def tile(t):
                        if t < TILES:
                            norm(t)
                        if t:
                            self.waits(eng, pe_h.at("routed", t - 1))
                            nc.vector.tensor_tensor(self.logits[:, t - 1], ps_r[:], rbias[:], ALU.add
                                                    ).then_inc(*dve_h.inc("logits"))

                    def norm(t):
                        u = t % 2
                        self.waits(eng, pe_t.at("out", t), (x_loaded[u], (t // 2 + 1) * 16),
                                   (x1_stored[u], t // 2 * 16))
                        nc.vector.tensor_tensor(x1[u][:], ps_out[:], x[u][:], ALU.add).then_inc(*dve_t.inc("x1"))
                        self.waits(eng, act_t.at("sq", t))
                        nc.vector.tensor_scalar(rq[:, u:u + 1], ss[:, u:u + 1], 1.0 / D, EPS_2, ALU.mult, ALU.add
                                                ).then_inc(*dve_t.inc("meansq"))
                        self.waits(eng, act_t.at("root", t))
                        nc.vector.reciprocal(rq[:, u:u + 1], rq[:, u:u + 1]).then_inc(*dve_t.inc("inv"))
                        self.waits(eng, dve_t.at("inv", t), (h2_stored[u], t // 2 * 16))
                        nc.vector.scalar_tensor_tensor(h2[u][:], x1[u][:], rq[:, u:u + 1], n2w[:], ALU.mult, ALU.mult
                                                       ).then_inc(*dve_t.inc("h2"))
                    add(0)
                    centre(0)
                    schedule(item, tile)

    def route(self):
        nc = self.nc
        XB = SEQ_P + SEQ_S
        NJ = (XB - 1) // P
        with ExitStack() as ctx:
            sb = lambda n, s, dt=F32: ctx.enter_context(nc.sbuf_tensor("q_" + n, s, dt))
            count_i = sb("count_i", [P, NE], I32)
            count, below = sb("count", [P, NE]), sb("below", [P, NE])
            limit = sb("limit", [P, NJ])
            token = [sb(f"token{k}", [P, TILES, 2], U32) for k in range(2)]
            unused = sb("unused", [P, NSLOT, 2], U32)
            block_i, blocks_f = sb("block_i", [P, NBLK], I32), sb("blocks_f", [P, NBLK])
            ended = sb("ended", [P, NBLK, NE])
            expert_f = sb("expert_f", [P, NBLK])
            begun, rounds_f = sb("begun", [P, NBLK // 2]), sb("rounds_f", [P, 1])
            strict = sb("strict", [P, P])
            ones = sb("ones", [P, NE])
            gmax, gmin, gsum, pg, inv, m1, m2, diff, e2, lowest = (
                sb(n, [P, TILES]) for n in ("gmax", "gmin", "gsum", "pg", "inv", "m1", "m2", "diff", "e2", "lowest"))
            gd, ge, gcand, goh = (sb(n, [P, TILES, NG]) for n in ("gd", "ge", "gcand", "goh"))
            mine = sb("mine", [P, TILES, NG, EG])
            elg, rest, cand = (sb(n, [P, TILES, EG]) for n in ("elg", "rest", "cand"))
            oh = [sb(f"oh{k}", [P, TILES, EG]) for k in range(2)]
            pick = [sb(f"pick{k}", [P, TILES, NG, EG]) for k in range(2)]
            picked = sb("picked", [P, TILES, NE])
            before = sb("before", [P, TILES + 1, NE])
            over = sb("over", [P, NE, NJ])
            dest = [sb(f"dest{k}", [P, TILES], U32) for k in range(2)]
            nb, end, base = (sb(n, [P, NE]) for n in ("nb", "end", "base"))
            pos = sb("pos", [P, TILES, NE])
            at_pos = [sb(f"at_pos{k}", [P, TILES, NE]) for k in range(2)]
            dest_f = [sb(f"dest_f{k}", [P, TILES]) for k in range(2)]
            ps_rank = ctx.enter_context(nc.psum_tensor("q_ps_rank", [P, TILES * NE], F32))
            ps_tot = ctx.enter_context(nc.psum_tensor("q_ps_tot", [P, TILES * NE], F32))
            pool = Marks(self.sem("q_pool"), "count token unused ones_done strict")
            dve = Marks(self.sem("q_dve"), "blocks count below limit ones gmax gd geq gcand gmin goh mine elg "
                        "m1 eq0 cand0 lowest0 oh0 rest m2 eq1 cand1 lowest1 oh1 diff gsum pg add inv g1 g2 "
                        "pick0 pick1 picked first " + " ".join(f"before{t}" for t in range(TILES)) +
                        " over nb nb1 end start base rank pos at0 at1 dest_f0 dest_f1 dest0 dest1 "
                        "ended expert_f last expert begun rounds_f rounds")
            act = Marks(self.sem("q_act"), "ge e2")
            pe = Marks(self.sem("q_pe"), "rank tot")
            cleared = self.sem("q_cleared")
            scattered = self.sem("q_scattered")
            groups = self.logits[:, :, 0:NG]
            experts = self.logits[:, :, NG:].rearrange("p t (g j) -> p t g j", g=NG)
            over_g = lambda ap: ap.unsqueeze(2).broadcast_to((P, TILES, NG, EG))
            over_j = lambda ap: ap.unsqueeze(3).broadcast_to((P, TILES, NG, EG))
            wide = lambda ap, n: ap.unsqueeze(2).broadcast_to((P, TILES, n))
            each_tile = lambda ap, n: ap.unsqueeze(1).broadcast_to((P, TILES, n))

            with nc.Block() as block:
                @block.sync
                def _(sp):
                    self.load_expert(sp, 0, 0)
                    self.waits(sp, pool.at("unused", 0))
                    with nc.allow_non_contiguous_dma(reason="pairs of indices"):
                        sp.dma_start(self.slots.rearrange("(b p) o -> p b o", p=P), unused[:]).then_inc(cleared, 16)

                @block.gpsimd
                def _(eng):
                    nc.gpsimd.iota(count_i[:], [[1, NE]], base=0, channel_multiplier=0)
                    nc.gpsimd.iota(block_i[:], [[1, NBLK]], base=0, channel_multiplier=0).then_inc(*pool.inc("count"))
                    for k in range(2):
                        nc.gpsimd.iota(token[k][:, :, 0], [[P, TILES]], base=0, channel_multiplier=1)
                        nc.gpsimd.iota(token[k][:, :, 1], [[P, TILES]], base=k * T, channel_multiplier=1)
                    nc.gpsimd.iota(unused[:, :, 1], [[0, NSLOT]], base=2 * T, channel_multiplier=1
                                   ).then_inc(*pool.inc("token"))
                    nc.gpsimd.memset(unused[:, :, 0], 0).then_inc(*pool.inc("unused"))
                    nc.gpsimd.memset(strict[:], 1.0).then_inc(*pool.inc("ones_done"))
                    self.waits(eng, pool.at("ones_done", 0))
                    nc.gpsimd.affine_select(out=strict[:], in_=strict[:], compare_op=ALU.is_gt, fill=0.0, base=0,
                                            pattern=[[1, P]], channel_multiplier=-1).then_inc(*pool.inc("strict"))
                    self.waits(eng, dve.at("dest1", 0), (cleared, 16))
                    for k in range(2):
                        for t in range(TILES):
                            nc.gpsimd.indirect_dma_start(
                                self.slots, bass.IndirectOffsetOnAxis(ap=dest[k][:, t:t + 1], axis=0),
                                token[k][:, t], None).then_inc(scattered, 16)
                    eng.wait_ge(scattered, 2 * TILES * 16)

                @block.scalar
                def _(eng):
                    self.waits(eng, dve.at("gd", 0))
                    nc.scalar.activation(ge[:], gd[:], ACT.Exp).then_inc(*act.inc("ge"))
                    self.waits(eng, dve.at("diff", 0))
                    nc.scalar.activation(e2[:], diff[:], ACT.Exp).then_inc(*act.inc("e2"))

                @block.tensor
                def _(eng):
                    self.waits(eng, dve.at("picked", 0), pool.at("strict", 0))
                    flat = picked[:].rearrange("p t e -> p (t e)")
                    nc.tensor.matmul(ps_rank[:], strict[:], flat, start=True, stop=True).then_inc(*pe.inc("rank"))
                    nc.tensor.matmul(ps_tot[:], self.allsum[:], flat, start=True, stop=True).then_inc(*pe.inc("tot"))

                @block.vector
                def _(eng):
                    v = nc.vector

                    def after(*names):
                        self.waits(eng, *(dve.at(n, 0) for n in names))
                    self.waits(eng, pool.at("token", 0))
                    v.tensor_copy(blocks_f[:], block_i[:]).then_inc(*dve.inc("blocks"))
                    v.tensor_copy(count[:], count_i[:]).then_inc(*dve.inc("count"))
                    after("count")
                    v.tensor_scalar(below[:], count[:], float(NE), None, ALU.subtract).then_inc(*dve.inc("below"))
                    v.tensor_scalar(limit[:], count[:, 0:NJ], float(P), float(P), ALU.mult, ALU.add
                                    ).then_inc(*dve.inc("limit"))
                    v.memset(ones[:], 1.0).then_inc(*dve.inc("ones"))
                    v.tensor_reduce(gmax[:], groups, AX_X, ALU.max).then_inc(*dve.inc("gmax"))
                    after("gmax")
                    v.tensor_tensor(gd[:], groups, wide(gmax[:], NG), ALU.subtract).then_inc(*dve.inc("gd"))
                    v.tensor_tensor(gcand[:], groups, wide(gmax[:], NG), ALU.is_equal).then_inc(*dve.inc("geq"))
                    after("geq")
                    v.tensor_tensor(gcand[:], gcand[:], each_tile(below[:, 0:NG], NG), ALU.mult
                                    ).then_inc(*dve.inc("gcand"))
                    after("gcand")
                    v.tensor_reduce(gmin[:], gcand[:], AX_X, ALU.min).then_inc(*dve.inc("gmin"))
                    after("gmin")
                    v.tensor_tensor(goh[:], gcand[:], wide(gmin[:], NG), ALU.is_equal).then_inc(*dve.inc("goh"))
                    after("goh")
                    v.tensor_tensor(mine[:], experts, over_j(goh[:]), ALU.mult).then_inc(*dve.inc("mine"))
                    after("mine")
                    v.tensor_reduce(elg[:], mine[:].rearrange("p t g j -> p t j g"), AX_X, ALU.add
                                    ).then_inc(*dve.inc("elg"))
                    after("elg")
                    for k, (val, top) in enumerate(((elg, m1), (rest, m2))):
                        v.tensor_reduce(top[:], val[:], AX_X, ALU.max).then_inc(*dve.inc(f"m{k + 1}"))
                        after(f"m{k + 1}")
                        v.tensor_tensor(cand[:], val[:], wide(top[:], EG), ALU.is_equal).then_inc(*dve.inc(f"eq{k}"))
                        after(f"eq{k}")
                        v.tensor_tensor(cand[:], cand[:], each_tile(below[:, 0:EG], EG), ALU.mult
                                        ).then_inc(*dve.inc(f"cand{k}"))
                        after(f"cand{k}")
                        v.tensor_reduce(lowest[:], cand[:], AX_X, ALU.min).then_inc(*dve.inc(f"lowest{k}"))
                        after(f"lowest{k}")
                        v.tensor_tensor(oh[k][:], cand[:], wide(lowest[:], EG), ALU.is_equal
                                        ).then_inc(*dve.inc(f"oh{k}"))
                        after(f"oh{k}")
                        if k == 0:
                            v.scalar_tensor_tensor(rest[:], oh[0][:], -3e38, elg[:], ALU.mult, ALU.add
                                                   ).then_inc(*dve.inc("rest"))
                            after("rest")
                    v.tensor_tensor(diff[:], m2[:], m1[:], ALU.subtract).then_inc(*dve.inc("diff"))
                    self.waits(eng, act.at("ge", 0))
                    v.tensor_reduce(gsum[:], ge[:], AX_X, ALU.add).then_inc(*dve.inc("gsum"))
                    after("gsum")
                    v.reciprocal(pg[:], gsum[:]).then_inc(*dve.inc("pg"))
                    self.waits(eng, act.at("e2", 0))
                    v.tensor_scalar(inv[:], e2[:], 1.0, None, ALU.add).then_inc(*dve.inc("add"))
                    after("add")
                    v.reciprocal(inv[:], inv[:]).then_inc(*dve.inc("inv"))
                    after("inv")
                    v.tensor_tensor(self.gate[0][:], pg[:], inv[:], ALU.mult).then_inc(*dve.inc("g1"))
                    after("g1")
                    v.tensor_tensor(self.gate[1][:], self.gate[0][:], e2[:], ALU.mult).then_inc(*dve.inc("g2"))
                    for k in range(2):
                        v.tensor_tensor(pick[k][:], over_j(goh[:]), over_g(oh[k][:]), ALU.mult
                                        ).then_inc(*dve.inc(f"pick{k}"))
                    after("pick1")
                    by_expert = lambda ap: ap.rearrange("p t g j -> p t (g j)")
                    v.tensor_tensor(picked[:], by_expert(pick[0][:]), by_expert(pick[1][:]), ALU.add
                                    ).then_inc(*dve.inc("picked"))
                    v.memset(before[:, 0], 0.0).then_inc(*dve.inc("first"))
                    self.waits(eng, pe.at("tot", 0))
                    tile = lambda ps, t: ps[:, t * NE:(t + 1) * NE]
                    for t in range(TILES):
                        after(f"before{t - 1}" if t else "first")
                        v.tensor_tensor(before[:, t + 1], before[:, t], tile(ps_tot, t), ALU.add
                                        ).then_inc(*dve.inc(f"before{t}"))
                    after(f"before{TILES - 1}")
                    v.tensor_tensor(over[:], before[:, TILES].unsqueeze(2).broadcast_to((P, NE, NJ)),
                                    limit[:].unsqueeze(1).broadcast_to((P, NE, NJ)), ALU.is_gt
                                    ).then_inc(*dve.inc("over"))
                    after("over")
                    v.tensor_reduce(nb[:], over[:], AX_X, ALU.add).then_inc(*dve.inc("nb"))
                    after("nb")
                    v.tensor_scalar(nb[:], nb[:], 1.0, None, ALU.add).then_inc(*dve.inc("nb1"))
                    after("nb1")
                    v.tensor_tensor_scan(end[:], ones[:], nb[:], 0.0, ALU.mult, ALU.add).then_inc(*dve.inc("end"))
                    after("end")
                    v.tensor_tensor(base[:], end[:], nb[:], ALU.subtract).then_inc(*dve.inc("start"))
                    after("start")
                    v.tensor_scalar(base[:], base[:], float(P), None, ALU.mult).then_inc(*dve.inc("base"))
                    v.tensor_tensor(pos[:], ps_rank[:].rearrange("p (t e) -> p t e", e=NE), before[:, 0:TILES], ALU.add
                                    ).then_inc(*dve.inc("rank"))
                    after("rank")
                    v.tensor_tensor(pos[:], pos[:], each_tile(base[:], NE), ALU.add).then_inc(*dve.inc("pos"))
                    after("pos")
                    for k in range(2):
                        v.tensor_tensor(at_pos[k][:], by_expert(pick[k][:]), pos[:], ALU.mult
                                        ).then_inc(*dve.inc(f"at{k}"))
                    for k in range(2):
                        after(f"at{k}")
                        v.tensor_reduce(dest_f[k][:], at_pos[k][:], AX_X, ALU.add).then_inc(*dve.inc(f"dest_f{k}"))
                    for k in range(2):
                        after(f"dest_f{k}")
                        v.tensor_copy(dest[k][:], dest_f[k][:]).then_inc(*dve.inc(f"dest{k}"))
                    v.tensor_tensor(ended[:], end[:].unsqueeze(1).broadcast_to((P, NBLK, NE)),
                                    blocks_f[:].unsqueeze(2).broadcast_to((P, NBLK, NE)), ALU.is_le
                                    ).then_inc(*dve.inc("ended"))
                    after("ended")
                    v.tensor_reduce(expert_f[:], ended[:], AX_X, ALU.add).then_inc(*dve.inc("expert_f"))
                    after("expert_f")
                    v.tensor_scalar(expert_f[:], expert_f[:], float(NE - 1), None, ALU.min).then_inc(*dve.inc("last"))
                    after("last")
                    v.tensor_copy(self.expert[:], expert_f[:]).then_inc(*dve.inc("expert"))
                    v.tensor_tensor(begun[:], end[:, NE - 1:NE].broadcast_to((P, NBLK // 2)), blocks_f[:, 0:NBLK:2],
                                    ALU.is_gt).then_inc(*dve.inc("begun"))
                    after("begun")
                    v.tensor_reduce(rounds_f[:], begun[:], AX_X, ALU.add).then_inc(*dve.inc("rounds_f"))
                    after("rounds_f")
                    v.tensor_copy(self.rounds[:], rounds_f[:]).then_inc(*dve.inc("rounds"))

    def load_expert(self, sp, e, u):
        for dst, name, k in ((self.wg, "moe_w_gate", KT), (self.wu, "moe_w_up", KT), (self.wd, "moe_w_down", KD)):
            src = self.a[name][0].rearrange("e (p c) n -> (e p) c n", c=k)[bass.ds(e * P, P)]
            sp.dma_start(dst[u][:], src).then_inc(self.w_loaded[u], 16)

    def experts(self):
        nc = self.nc
        with ExitStack() as ctx:
            sb = lambda n, s, dt=F32: ctx.enter_context(nc.sbuf_tensor("e_" + n, s, dt))
            psum = lambda n, w: ctx.enter_context(nc.psum_tensor("e_ps_" + n, [P, w], F32))
            wg, wu, wd = self.wg, self.wu, self.wd
            slots = sb("slots", [P, NSLOT, 2], U32)
            idx = [sb(f"idx{u}", [P, 1], U32) for u in range(2)]
            row = [sb(f"row{u}", [P, 1], U32) for u in range(2)]
            x, xT, y = ([sb(f"{n}{u}", [P, D]) for u in range(2)] for n in ("x", "xT", "y"))
            silu, hid = sb("silu", [P, DE]), [sb(f"hid{u}", [P, DE]) for u in range(2)]
            ps_g, ps_u, ps_t, ps_y = psum("g", DE), psum("u", DE), psum("t", D), psum("y", D)
            slots_loaded = self.sem("e_slots_loaded")
            idx_made = self.sem("e_idx_made")
            row_made = self.sem("e_row_made")
            y_free = self.sem("e_y_free")
            x_loaded = [self.sem(f"e_x_loaded{u}") for u in range(2)]
            y_stored = self.sem("e_y_stored")
            pe_x = Marks(self.sem("e_pe_x"), "turned")
            pe = Marks(self.sem("e_pe"), "gate up down", base=6)
            act_x = Marks(self.sem("e_act_x"), "turned")
            act = Marks(self.sem("e_act"), "silu y", base=2)
            dve = Marks(self.sem("e_dve"), "hid y", base=2)
            dve_x = Marks(self.sem("e_dve_x"), "turned")

            def blocks(eng, body):
                rounds = eng.value_load(self.rounds[0:1, 0:1], min_val=1, max_val=NBLK // 2)
                with eng.Fori(0, rounds) as half:
                    for u in range(2):
                        body(half * 2 + u, u, half)
                return rounds

            with nc.Block() as block:
                @block.sync
                def _(sp):
                    second = sp.value_load(self.expert[0:1, 1:2], min_val=0, max_val=NE - 1)
                    self.load_expert(sp, second, 1)
                    rounds = sp.value_load(self.rounds[0:1, 0:1], min_val=1, max_val=NBLK // 2)
                    with sp.Fori(1, rounds) as half:
                        for u in range(2):
                            b = half * 2 + u
                            e = sp.value_load(self.expert[0:1, bass.ds(b, 1)], min_val=0, max_val=NE - 1)
                            self.hold_sp(sp, pe.at("down", b - 2))
                            self.load_expert(sp, e, u)

                @block.gpsimd
                def _(eng):
                    with nc.allow_non_contiguous_dma(reason="pairs of indices"):
                        eng.dma_start(slots[:], self.slots.rearrange("(b p) o -> p b o", p=P)
                                      ).then_inc(slots_loaded, 16)
                    eng.wait_ge(slots_loaded, 16)

                    def gather(b, u):
                        nc.gpsimd.tensor_copy(idx[u][:], slots[:, bass.ds(b, 1), 0]).then_inc(idx_made, 1)
                        self.waits(eng, (idx_made, b + 1))
                        eng.sem_inc(self.pool_turn, 1)
                        nc.gpsimd.indirect_dma_start(
                            x[u][:], None, self.h2, bass.IndirectOffsetOnAxis(ap=idx[u][:, 0:1], axis=0)
                        ).then_inc(x_loaded[u], 16)

                    gather(0, 0)
                    gather(1, 1)
                    eng.sem_inc(y_free, 2)
                    self.waits(eng, pe_x.at("turned", 0))
                    gather(2, 0)

                    def body(b, u, half):
                        nc.gpsimd.tensor_copy(row[u][:], slots[:, bass.ds(b, 1), 1]).then_inc(row_made, 1)
                        self.waits(eng, (row_made, b + 1), act.at("y", b), dve.at("y", b))
                        eng.sem_inc(self.pool_turn, 1)
                        nc.gpsimd.indirect_dma_start(
                            self.ytok, bass.IndirectOffsetOnAxis(ap=row[u][:, 0:1], axis=0), y[u][:], None
                        ).then_inc(y_stored, 16)
                        self.waits(eng, pe_x.at("turned", b + 1))
                        eng.sem_inc(self.pool_turn, 1)
                        gather(b + 3, 1 - u)
                        self.waits(eng, (y_stored, b * 16 + 16))
                        eng.sem_inc(y_free, 1)
                    rounds = blocks(eng, body)
                    self.waits(eng, (x_loaded[0], rounds * 16 + 32), (x_loaded[1], rounds * 16 + 16))
                    eng.sem_inc(self.pool_turn, 1)

                @block.tensor
                def _(eng):
                    eng.sem_inc(pe.sem, 6)

                    def turn(b, u, half):
                        self.hold_pe(eng, (x_loaded[u], half * 16 + 16),
                                     None if isinstance(b, int) else act_x.at("turned", b - 1),
                                     None if isinstance(b, int) else dve_x.at("turned", b - 1))
                        for c in range(KT):
                            last = nc.tensor.transpose(ps_t[:, c * P:(c + 1) * P], x[u][:, c:D:KT], self.ident[:])
                        last.then_inc(*pe_x.inc("turned"))
                    turn(0, 0, 0)

                    def body(b, u, half):
                        self.hold_pe(eng, act_x.at("turned", b), dve_x.at("turned", b),
                                     (self.w_loaded[u], half * 48 + 48))
                        for name, w, ps in (("gate", wg, ps_g), ("up", wu, ps_u)):
                            for q in range(KD):
                                for c in range(KT):
                                    last = nc.tensor.matmul(ps[:, q * P:(q + 1) * P], w[u][:, c, q:DE:KD],
                                                            xT[u][:, c * P:(c + 1) * P], start=c == 0,
                                                            stop=c == KT - 1)
                            last.then_inc(*pe.inc(name))
                        turn(b + 1, 1 - u, half + u)
                        self.hold_pe(eng, dve.at("hid", b), act.at("y", b - 1), dve.at("y", b - 1))
                        for n in range(2):
                            for q in range(KD):
                                last = nc.tensor.matmul(ps_y[:, n * 512:(n + 1) * 512], hid[u][:, q * P:(q + 1) * P],
                                                        wd[u][:, q, n * 512:(n + 1) * 512],
                                                        start=q == 0, stop=q == KD - 1)
                        last.then_inc(*pe.inc("down"))
                    blocks(eng, body)

                @block.scalar
                def _(eng):
                    eng.sem_inc(act.sem, 2)

                    def turn(b, u):
                        self.waits(eng, pe_x.at("turned", b), pe.at("up", b - 2))
                        nc.scalar.activation(xT[u][:, 0:512], ps_t[:, 0:512], ACT.Copy).then_inc(*act_x.inc("turned"))
                    turn(0, 0)

                    def body(b, u, half):
                        self.waits(eng, pe.at("gate", b), dve.at("hid", b - 1))
                        nc.scalar.activation(silu[:], ps_g[:], ACT.Silu).then_inc(*act.inc("silu"))
                        turn(b + 1, 1 - u)
                        self.waits(eng, pe.at("down", b), (y_free, b + 1))
                        nc.scalar.activation(y[u][:, 0:512], ps_y[:, 0:512], ACT.Copy).then_inc(*act.inc("y"))
                    blocks(eng, body)

                @block.vector
                def _(eng):
                    eng.sem_inc(dve.sem, 2)

                    def turn(b, u):
                        self.waits(eng, pe_x.at("turned", b), pe.at("up", b - 2))
                        nc.vector.tensor_copy(xT[u][:, 512:], ps_t[:, 512:]).then_inc(*dve_x.inc("turned"))
                    turn(0, 0)

                    def body(b, u, half):
                        self.waits(eng, pe.at("up", b), act.at("silu", b), pe.at("down", b - 2))
                        nc.vector.tensor_tensor(hid[u][:], ps_u[:], silu[:], ALU.mult).then_inc(*dve.inc("hid"))
                        turn(b + 1, 1 - u)
                        self.waits(eng, pe.at("down", b), (y_free, b + 1))
                        nc.vector.tensor_copy(y[u][:, 512:], ps_y[:, 512:]).then_inc(*dve.inc("y"))
                    blocks(eng, body)

    def combine(self):
        nc = self.nc
        EPS = 1e-6
        with ExitStack() as ctx:
            sb = lambda n, s, dt=F32: ctx.enter_context(nc.sbuf_tensor("c_" + n, s, dt))
            AHEAD = 4
            y = [[sb(f"y{k}{u}", [P, D]) for u in range(AHEAD)] for k in range(2)]
            x1 = [sb(f"x1{u}", [P, D]) for u in range(AHEAD)]
            out, junk = ([sb(f"{n}{u}", [P, D]) for u in range(2)] for n in ("out", "junk"))
            fw = sb("fw", [P, D])
            ss, rq = sb("ss", [P, TILES]), sb("rq", [P, TILES])
            fw_loaded = self.sem("c_fw_loaded")
            x_loaded = [self.sem(f"c_x_loaded{u}") for u in range(AHEAD)]
            stored = [self.sem(f"c_stored{u}") for u in range(2)]
            act = Marks(self.sem("c_act"), "sq root")
            dve = Marks(self.sem("c_dve"), "one two meansq inv out")

            with nc.Block() as block:
                @block.sync
                def _(sp):
                    sp.dma_start(fw[:], self.a["final_norm_w"].partition_broadcast(P)).then_inc(fw_loaded, 16)

                    def load(t):
                        u = t % AHEAD
                        self.waits(sp, dve.ago("out", t, AHEAD))
                        sp.dma_start(x1[u][:], self.x1[t * P:(t + 1) * P]).then_inc(x_loaded[u], 16)
                        for k in range(2):
                            sp.dma_start(y[k][u][:], self.ytok[k * T + t * P:k * T + (t + 1) * P]
                                         ).then_inc(x_loaded[u], 16)
                    for t in range(AHEAD - 1):
                        load(t)
                    for t in range(TILES):
                        if t + AHEAD - 1 < TILES:
                            load(t + AHEAD - 1)
                        self.waits(sp, dve.at("out", t))
                        row = t * P if t * P < SEQ_P else t * P - SEQ_P
                        sp.dma_start(self.outs[int(t * P >= SEQ_P)][0, row:row + P], out[t % 2][:]
                                     ).then_inc(stored[t % 2], 16)
                    for u in range(2):
                        sp.wait_ge(stored[u], TILES // 2 * 16)

                @block.scalar
                def _(eng):
                    for t in range(TILES):
                        u = t % 2
                        self.waits(eng, dve.at("two", t), dve.ago("out", t, 2))
                        if t >= 2:
                            self.waits(eng, act.at("sq", t - 2))
                        nc.scalar.activation(junk[u][:], x1[t % AHEAD][:], ACT.Square, accum_out=ss[:, t:t + 1]
                                             ).then_inc(*act.inc("sq"))
                        self.waits(eng, dve.at("meansq", t))
                        nc.scalar.activation(rq[:, t:t + 1], ss[:, t:t + 1], ACT.Sqrt).then_inc(*act.inc("root"))

                @block.vector
                def _(eng):
                    eng.wait_ge(fw_loaded, 16)
                    for t in range(TILES):
                        u = t % 2
                        w = t % AHEAD
                        x = x1[w][:]
                        self.waits(eng, (x_loaded[w], (t // AHEAD + 1) * 48))
                        nc.vector.scalar_tensor_tensor(x, y[0][w][:], self.gate[0][:, t:t + 1], x, ALU.mult, ALU.add
                                                       ).then_inc(*dve.inc("one"))
                        self.waits(eng, dve.at("one", t))
                        nc.vector.scalar_tensor_tensor(x, y[1][w][:], self.gate[1][:, t:t + 1], x, ALU.mult, ALU.add
                                                       ).then_inc(*dve.inc("two"))
                        self.waits(eng, act.at("sq", t))
                        nc.vector.tensor_scalar(ss[:, t:t + 1], ss[:, t:t + 1], 1.0 / D, EPS, ALU.mult, ALU.add
                                                ).then_inc(*dve.inc("meansq"))
                        self.waits(eng, act.at("root", t))
                        nc.vector.reciprocal(rq[:, t:t + 1], rq[:, t:t + 1]).then_inc(*dve.inc("inv"))
                        self.waits(eng, dve.at("inv", t), (stored[u], t // 2 * 16))
                        nc.vector.scalar_tensor_tensor(out[u][:], x, rq[:, t:t + 1], fw[:], ALU.mult, ALU.mult
                                                       ).then_inc(*dve.inc("out"))


_INS = ["x_prompt", "x_sample", "norm1_w", "w_in", "mu_shift", "rwkv_w0", "rwkv_w2", "rwkv_a0", "rwkv_a2", "rwkv_g2",
        "rwkv_k_k", "rwkv_k_a", "rwkv_r_k", "rwkv_lnx_w", "rwkv_lnx_b", "hgrn_lb", "hgrn_gnorm_w", "w_out", "norm2_w",
        "router_group_w", "router_group_b", "router_expert_w", "router_expert_b", "moe_w_gate", "moe_w_up",
        "moe_w_down", "final_norm_w"]
_OUTS = [(1, SEQ_P, D), (1, SEQ_S, D)]


def kernel(**inputs):
    import concourse.bacc as _bacc
    from concourse.bass_utils import run_bass_kernel_spmd as _run

    nc = _bacc.Bacc("TRN2", target_bir_lowering=False, num_devices=1)
    arrays, args = {}, {}
    for name in _INS:
        arr = np.ascontiguousarray(inputs[name])
        arrays[f"in_{name}_dram"] = arr
        args[name] = nc.dram_tensor(f"in_{name}_dram", arr.shape, mybir.dt.from_np(arr.dtype),
                                    kind="ExternalInput").ap()
    outs = [nc.dram_tensor(f"out_{i}_dram", shape, F32, kind="ExternalOutput").ap() for i, shape in enumerate(_OUTS)]
    Kernel(nc, args, outs, 9).build()
    r = _run(nc, [arrays], core_ids=[0])
    return tuple(r.results[0][f"out_{i}_dram"] for i in range(len(_OUTS)))
```
